# Optimizing a Trainium2 kernel written in Bass

```python
import math
import jax, jax.numpy as jnp
from jax import lax
import numpy as np

D_MODEL = 1024
BATCH = 1
SEQ = 2048
DEPTH = 1
DEC_BATCH = 1
DEC_SEQ = 32
PAST_LEN = 1024

CHUNK = 64
MIX_WIDTH = D_MODEL
D_POOL = MIX_WIDTH // 2
POOL_WINDOWS = (2, 4, 8, 16)
POOL_GROUPS = len(POOL_WINDOWS)
POOL_GC = D_POOL // POOL_GROUPS
POOL_HIST = max(POOL_WINDOWS) - 1
D_ATTN = MIX_WIDTH - D_POOL
HEAD_DIM = 64
N_HEADS = D_ATTN // HEAD_DIM
N_KV_HEADS = 2
KV_GROUP = N_HEADS // N_KV_HEADS
N_IDX_HEADS = 8
D_IDX = 32
TOPK_MAX = 256
Q_BLOCK = 128
NUM_BUCKETS = 32
MAX_DISTANCE = 1024
EPS = 1e-6
ATTN_SCALE = HEAD_DIM ** -0.5
INDEX_SCALE = (D_IDX ** -0.5) * (N_IDX_HEADS ** -0.5)

_IN_SIZES = (D_POOL, D_POOL, N_HEADS * HEAD_DIM, N_KV_HEADS * HEAD_DIM, N_KV_HEADS * HEAD_DIM,
             N_IDX_HEADS * D_IDX, D_IDX, N_IDX_HEADS, D_ATTN)
IN_COLS = sum(_IN_SIZES)
_SPLITS = tuple(int(s) for s in np.cumsum(_IN_SIZES)[:-1])

kernel_name = "hybrid_pool_dsa_streaming_step"

def _rmsnorm(x, g):
    xf = x.astype(jnp.float32)
    y = xf * lax.rsqrt(jnp.mean(xf * xf, axis=-1, keepdims=True) + EPS) * g.astype(jnp.float32)
    return y.astype(x.dtype)

def _t5_bucket(rel):
    nb = NUM_BUCKETS // 2
    max_exact = nb // 2
    ret = (rel > 0).astype(jnp.int32) * nb
    n = jnp.abs(rel)
    nf = jnp.maximum(n, 1).astype(jnp.float32)
    large = max_exact + (jnp.log(nf / max_exact) / math.log(MAX_DISTANCE / max_exact)
                         * (nb - max_exact)).astype(jnp.int32)
    large = jnp.minimum(large, nb - 1)
    return ret + jnp.where(n < max_exact, n, large)

def _pool_mixer(u, hist, pos0, w_pool, pool_scale):
    B, L, C = u.shape
    P = POOL_HIST
    ext = jnp.concatenate([hist, u], axis=1).astype(jnp.float32)
    cs = jnp.concatenate([jnp.zeros((B, 1, C), jnp.float32), jnp.cumsum(ext, axis=1)], axis=1)
    pos = pos0 + jnp.arange(L, dtype=jnp.int32)
    pooled = []
    for g, w in enumerate(POOL_WINDOWS):
        sl = slice(g * POOL_GC, (g + 1) * POOL_GC)
        s = cs[:, P + 1:P + 1 + L, sl] - cs[:, P + 1 - w:P + 1 - w + L, sl]
        cnt = jnp.minimum(w, pos + 1).astype(jnp.float32)
        pooled.append(s / cnt[None, :, None])
    pooled = jnp.concatenate(pooled, axis=-1)
    d = (pooled - ext[:, P:]).reshape(B, L, POOL_GROUPS, POOL_GC)
    y = jnp.einsum('blgc,gcd->blgd', d, w_pool.astype(jnp.float32)).reshape(B, L, C)
    y = y * pool_scale.astype(jnp.float32)
    return y.astype(u.dtype), ext[:, -P:].astype(u.dtype)

def _dsa_attention(q, qi, wi, k_all, v_all, ki_all, pos0, rel_bias):
    B, Lq = q.shape[:2]
    Lk = k_all.shape[1]
    topk = min(TOPK_MAX, Lk // 4)
    qb = min(Q_BLOCK, Lq)
    nb = Lq // qb
    key_chunk = jnp.arange(Lk, dtype=jnp.int32) // CHUNK
    ki_f = ki_all.astype(jnp.float32)
    gather = jax.vmap(lambda arr, idx: arr[idx])

    def block(args):
        qblk, qiblk, wiblk, qpos = args
        qchunk = qpos // CHUNK
        dots = jnp.einsum('bqhd,bkd->bqhk', qiblk.astype(jnp.float32), ki_f)
        score = jnp.einsum('bqh,bqhk->bqk', wiblk.astype(jnp.float32), jax.nn.relu(dots)) * INDEX_SCALE
        vis = key_chunk[None, :] <= qchunk[:, None]
        score = jnp.where(vis[None], score, -jnp.inf)
        _, sel = lax.top_k(score, topk)
        valid = (sel // CHUNK) <= qchunk[None, :, None]
        ks = gather(k_all, sel).astype(jnp.float32)
        vs = gather(v_all, sel).astype(jnp.float32)
        bias = rel_bias.astype(jnp.float32)[_t5_bucket(sel - qpos[None, :, None])]
        bias = bias.reshape(B, qb, topk, N_KV_HEADS, KV_GROUP).transpose(0, 1, 3, 4, 2)
        qg = qblk.astype(jnp.float32).reshape(B, qb, N_KV_HEADS, KV_GROUP, HEAD_DIM)
        logits = jnp.einsum('bqgrd,bqkgd->bqgrk', qg, ks) * ATTN_SCALE + bias
        logits = jnp.where(valid[:, :, None, None, :], logits, -jnp.inf)
        p = jax.nn.softmax(logits, axis=-1)
        o = jnp.einsum('bqgrk,bqkgd->bqgrd', p, vs).reshape(B, qb, N_HEADS * HEAD_DIM)
        return o.astype(q.dtype)

    def to_blocks(a):
        return a.reshape((B, nb, qb) + a.shape[2:]).swapaxes(0, 1)

    qpos_all = (pos0 + jnp.arange(Lq, dtype=jnp.int32)).reshape(nb, qb)
    out = lax.map(block, (to_blocks(q), to_blocks(qi), to_blocks(wi), qpos_all))
    return out.swapaxes(0, 1).reshape(B, Lq, N_HEADS * HEAD_DIM)

def _layer(x, pool_hist, cache_k, cache_v, cache_kidx, pos0, rel_bias,
           g_pre, w_in, w_pool, pool_scale, w_out, g_post):
    B, L, _ = x.shape
    h = _rmsnorm(x, g_pre)
    proj = jnp.einsum('bld,de->ble', h, w_in)
    u_a, gate_a, q, k, v, qi, ki, wi, gate_b = jnp.split(proj, _SPLITS, axis=-1)
    y_a, new_pool = _pool_mixer(u_a, pool_hist, pos0, w_pool, pool_scale)
    q = q.reshape(B, L, N_HEADS, HEAD_DIM)
    k = k.reshape(B, L, N_KV_HEADS, HEAD_DIM)
    v = v.reshape(B, L, N_KV_HEADS, HEAD_DIM)
    qi = qi.reshape(B, L, N_IDX_HEADS, D_IDX)
    if cache_k is None:
        k_all, v_all, ki_all = k, v, ki
    else:
        k_all = jnp.concatenate([cache_k.astype(k.dtype), k], axis=1)
        v_all = jnp.concatenate([cache_v.astype(v.dtype), v], axis=1)
        ki_all = jnp.concatenate([cache_kidx.astype(ki.dtype), ki], axis=1)
    y_b = _dsa_attention(q, qi, wi, k_all, v_all, ki_all, pos0, rel_bias)
    mixed = jnp.concatenate([y_a * jax.nn.silu(gate_a), y_b * jax.nn.silu(gate_b)], axis=-1)
    out = jnp.einsum('ble,ed->bld', mixed, w_out)
    return x + _rmsnorm(out, g_post), k, v, ki, new_pool

def setup_inputs(seed: int = 0) -> dict:
    key = jax.random.key(seed)
    ks = jax.random.split(key, 16)
    f32 = jnp.float32
    return {
        "x_prompt": jax.random.normal(ks[0], (BATCH, SEQ, D_MODEL), f32),
        "x_sample": jax.random.normal(ks[1], (DEC_BATCH, DEC_SEQ, D_MODEL), f32),
        "cache_k": jax.random.normal(ks[2], (DEPTH, DEC_BATCH, PAST_LEN, N_KV_HEADS, HEAD_DIM), f32),
        "cache_v": jax.random.normal(ks[3], (DEPTH, DEC_BATCH, PAST_LEN, N_KV_HEADS, HEAD_DIM), f32),
        "cache_kidx": jax.random.normal(ks[4], (DEPTH, DEC_BATCH, PAST_LEN, D_IDX), f32),
        "state_pool": jax.random.normal(ks[5], (DEPTH, DEC_BATCH, POOL_HIST, D_POOL), f32),
        "rel_bias": 0.5 * jax.random.normal(ks[6], (NUM_BUCKETS, N_HEADS), f32),
        "g_pre": 1.0 + 0.01 * jax.random.normal(ks[7], (DEPTH, D_MODEL), f32),
        "w_in": jax.random.normal(ks[8], (DEPTH, D_MODEL, IN_COLS), f32) * D_MODEL ** -0.5,
        "w_pool": jax.random.normal(ks[9], (DEPTH, POOL_GROUPS, POOL_GC, POOL_GC), f32) * POOL_GC ** -0.5,
        "pool_scale": 1.0 + 0.01 * jax.random.normal(ks[10], (DEPTH, D_POOL), f32),
        "w_out": jax.random.normal(ks[11], (DEPTH, MIX_WIDTH, D_MODEL), f32) * MIX_WIDTH ** -0.5,
        "g_post": 1.0 + 0.01 * jax.random.normal(ks[12], (DEPTH, D_MODEL), f32),
    }

def reference(x_prompt, x_sample, cache_k, cache_v, cache_kidx, state_pool, rel_bias,
              g_pre, w_in, w_pool, pool_scale, w_out, g_post):
    past_len = cache_k.shape[2]
    hp = x_prompt
    hs = x_sample
    kp, vp, kip, pp = [], [], [], []
    kS, vS, kiS, pS = [], [], [], []
    zero_hist = jnp.zeros((x_prompt.shape[0], POOL_HIST, D_POOL), x_prompt.dtype)
    for l in range(DEPTH):
        hp, k1, v1, ki1, p1 = _layer(hp, zero_hist, None, None, None, 0, rel_bias,
                                     g_pre[l], w_in[l], w_pool[l], pool_scale[l], w_out[l], g_post[l])
        kp.append(k1); vp.append(v1); kip.append(ki1); pp.append(p1)
        hs, k2, v2, ki2, p2 = _layer(hs, state_pool[l].astype(x_sample.dtype), cache_k[l], cache_v[l],
                                     cache_kidx[l], past_len, rel_bias,
                                     g_pre[l], w_in[l], w_pool[l], pool_scale[l], w_out[l], g_post[l])
        kS.append(k2); vS.append(v2); kiS.append(ki2); pS.append(p2)
    return (hp, hs,
            jnp.stack(kp), jnp.stack(vp), jnp.stack(kip), jnp.stack(pp),
            jnp.stack(kS), jnp.stack(vS), jnp.stack(kiS), jnp.stack(pS))


_drawn_inputs = setup_inputs


def setup_inputs(seed=0):
    import zlib

    import numpy as np

    out = dict(_drawn_inputs(seed))
    spreads = {}
    factors = {}
    for name, (base, spread) in spreads.items():
        noise = np.random.default_rng([zlib.crc32(name.encode()), seed]).standard_normal(out[name].shape)
        drawn = base * np.exp(spread * noise) if base else spread * noise
        out[name] = __import__('jax').numpy.asarray(drawn.astype(out[name].dtype))
    for name, factor in factors.items():
        out[name] = (out[name] * factor).astype(out[name].dtype)
    return out
```

```python
from contextlib import ExitStack

import numpy as np
import concourse.bass as bass
from concourse import mybir

ALU = mybir.AluOpType
ACT = mybir.ActivationFunctionType
AX = mybir.AxisListType
F32 = mybir.dt.float32
F32R = mybir.dt.float32r
BF16 = mybir.dt.bfloat16
F16 = mybir.dt.float16
I32 = mybir.dt.int32
U32 = mybir.dt.uint32

P = 128
D = 1024
DC = D // P
SEQ, DEC, PAST = 2048, 32, 1024
CHUNK = 64
NPT = SEQ // P
ST = NPT
NT = NPT + 1
TOKENS = NT * P
DPOOL, NG = 512, 4
HIST = 15
UOFF = 16
NH, HD, NKV, GRP = 8, 64, 2, 4
NIH, DI = 8, 32
TOPK = 256
NBUCKETS = 32
EPS = 1e-6
ATTN_SCALE = HD ** -0.5
INDEX_SCALE = (DI ** -0.5) * (NIH ** -0.5)
C_U, C_GA, C_Q, C_K, C_V, C_QI, C_KI, C_WI, C_GB = 0, 512, 1024, 1536, 1664, 1792, 2048, 2080, 2088
COLS = 2600
BIAS_TILES = 6
BIAS_W = BIAS_TILES * P
GLEN = BIAS_W + P - 1
MASKED = -1e30
UNSEEN = -2.0
LEAST = -3e38
ROUNDS = (11, 11, 6)
ZOOM = 1024
SPAN = 15360.0
REACH = 16384.0
MAGIC = float(0x5F3759DF)

BLOCKS = [(4 * b, 4) for b in range(NPT // 4)] + [(ST, 1)]


def key_tiles(t):
    return t + 1 if t < NPT else PAST // P + 1


def place_of(t):
    return t if t < NPT else PAST // P


def score_chunks(t):
    n = key_tiles(t) * P
    return [(a, min(a + 1024, n)) for a in range(0, n, 1024)]


def phase1_steps():
    steps = [("N", 0), ("N", 1), ("N", 2)]
    pending = []

    def spread(k):
        for _ in range(min(k, len(pending))):
            steps.append(pending.pop(0))

    windows = []

    def pool_part():
        while windows:
            b, g = windows.pop(0)
            steps.append(("PD", b, g))
            steps.append(("PL", b, g))

    for b, (t0, nt) in enumerate(BLOCKS):
        for i in range(nt):
            steps.append(("H", t0 + i))
            spread(2)
            if i == 0 and nt == 4:
                steps.append(("N", t0 + 3))
        ahead = [BLOCKS[b + 1][0] + i for i in range(min(3, BLOCKS[b + 1][1]))] if b + 1 < len(BLOCKS) else []
        if nt == 1:
            spread(100)
            pool_part()
            steps.append(("HIST",))
            for j in range(PAST // P):
                steps.append(("KC", j))
        for i in range(nt):
            t = t0 + i
            k = -(-len(pending) // 6)
            steps.append(("TM", t))
            spread(k)
            for g in ([i] if nt == 4 else range(NG)):
                steps.append(("GB", b, g))
            pool_part()
            spread(k)
            if ahead:
                steps.append(("N", ahead.pop(0)))
            gs = [i] if nt == 4 else range(NG)
            for g in gs:
                steps.append(("Q", b, g))
                spread(k)
                if nt == 1:
                    pool_part()
                steps.append(("GA", b, g))
                spread(k)
                steps.append(("U", b, g))
                spread(k)
                windows.append((b, g))
            spread(100)
            steps.append(("TR", t))
            pending += [("I", t, h, c) for h in range(NIH) for c in range(len(score_chunks(t)))]
        if b >= len(BLOCKS) - 2:
            steps.append(("NP", b))
    pool_part()
    spread(100)
    return steps


def number(steps):
    fa, fg, fd, fi = {}, {}, {}, {}
    for s in steps:
        k = s[0]
        if k == "H":
            fa["H", s[1], 0] = len(fa)
            fa["H", s[1], 1] = len(fa)
        elif k == "TM":
            fa["TM", s[1], 0] = len(fa)
            fa["TM", s[1], 1] = len(fa)
        elif k in ("Q", "U"):
            fa[s] = len(fa)
        elif k in ("GB", "GA"):
            fg[s] = len(fg)
        elif k == "TR":
            for i in range(3):
                fd["TR", s[1], i] = len(fd)
        elif k in ("PL", "KC", "HIST", "NP"):
            fd[s] = len(fd)
        elif k == "I":
            fi[s] = len(fi)
    return fa, fg, fd, fi


def build(nc, A):
    ctx = ExitStack()
    with ctx:
        keep = {}

        def sb(stack, name, shape, dt):
            return stack.enter_context(nc.sbuf_tensor(name, shape, dt))

        def sem(name):
            return ctx.enter_context(nc.semaphore(name))

        def dram(name, shape):
            return nc.dram_tensor(name, shape, F32, kind="Internal").ap()

        q_dram = dram("q_scratch", (P, GRP, TOKENS))
        gb_dram = dram("gb_scratch", (P, GRP, TOKENS))

        ma_dram = dram("ma_scratch", (P, NG, TOKENS))
        s_dram = dram("s_scratch", (NT, P, SEQ))
        g_dram = dram("bias_scratch", (NH, P, GLEN))
        k_dram = dram("sample_keys_scratch", (NKV, P, PAST + P))

        identf = sb(ctx, "identf", [P, P], F32)
        identb = sb(ctx, "identb", [P, P], BF16)
        onesb = sb(ctx, "onesb", [P, P], BF16)
        kT = sb(ctx, "kT", [P, SEQ], F32)
        top = sb(ctx, "top", [P, NT], F32)

        banks = [ctx.enter_context(nc.psum_tensor(f"bank{i}", [P, 512], F32)) for i in range(4)]
        wide = [ctx.enter_context(nc.psum_tensor(f"wide{i}", [P, 1024], F32)) for i in range(2)]

        phase1(nc, A, sb, sem, identf, identb, onesb, kT, top, banks, wide, q_dram, gb_dram, ma_dram, s_dram)
        phase2(nc, A, sb, sem, identf, identb, onesb, kT, top, banks, wide, q_dram, gb_dram, ma_dram, s_dram,
               g_dram, k_dram)


def inverse_root(dve, done, n, ms, y, tmp, ss, scale):
    dve.tensor_scalar(ms, ss, scale, EPS, ALU.mult, ALU.add).then_inc(done, 1)
    n += 1
    dve.wait_ge(done, n)
    dve.tensor_scalar(y.bitcast(I32), ms.bitcast(I32), -0.5, MAGIC, ALU.mult, ALU.add).then_inc(done, 1)
    n += 1
    for _ in range(3):
        dve.wait_ge(done, n)
        dve.tensor_tensor(tmp, y, ms, ALU.mult).then_inc(done, 1)
        n += 1
        dve.wait_ge(done, n)
        dve.scalar_tensor_tensor(tmp, tmp, -0.5, y, ALU.mult, ALU.mult).then_inc(done, 1)
        n += 1
        dve.wait_ge(done, n)
        dve.scalar_tensor_tensor(y, tmp, 1.5, y, ALU.add, ALU.mult).then_inc(done, 1)
        n += 1
    dve.wait_ge(done, n)
    return n


def phase1(nc, A, sb, sem, identf, identb, onesb, kT, top, banks, wide, q_dram, gb_dram, ma_dram, s_dram):
    steps = phase1_steps()
    fa, fg, fd, fi = number(steps)
    norm_order = {s[1]: i for i, s in enumerate(x for x in steps if x[0] == "N")}
    pool_order = {s[1:]: i for i, s in enumerate(x for x in steps if x[0] == "PL")}
    with ExitStack() as st:
        W = sb(st, "W", [P, DC, COLS], F32)
        gpre = sb(st, "gpre", [P, DC], F32)
        pscale = sb(st, "pscale", [P, NG], F32)
        wpool = sb(st, "wpool", [P, NG, P], F32)
        fix = sb(st, "fix", [P, NG, 16], F32)
        xs = sb(st, "xs", [P, 3, D], F32)
        junk = sb(st, "junk", [P, D], BF16)
        ss = sb(st, "ss", [P, NT], F32)
        small = sb(st, "small", [P, 4], F32)
        hT = sb(st, "hT", [P, DC, 512], F32)
        kq = sb(st, "kq", [P, 2, 552], F32)
        qs = sb(st, "qs", [P, NIH, 3 * DI], F32)
        ks = sb(st, "ks", [P, 3 * DI], F32)
        wi = sb(st, "wi", [P, 2, NIH], F32)
        qiT = sb(st, "qiT", [3 * DI, 2, NIH, P], F32R)
        kiT = sb(st, "kiT", [3 * DI, SEQ], F32R)
        relu = sb(st, "relu", [P, 2, 1024], F32)
        S = sb(st, "S", [P, 2, SEQ], F32)
        gst = sb(st, "gst", [P, 2, 512], F32)
        sga = sb(st, "sga", [P, 2, 512], F32)
        qst = sb(st, "qst", [P, 2, 512], F32)
        U = sb(st, "U", [P, NG, UOFF + 512], F32)
        win = sb(st, "win", [P, 2, UOFF + 512], F32)
        kc = sb(st, "kc", [P, PAST // P, DI], F32)
        rows = sb(st, "rows", [HIST, DPOOL], F32)

        x_in = [sem(f"x_in{i}") for i in range(3)]
        wa_in = [sem(f"wa_in{c}") for c in range(DC)]
        wb_in = [sem(f"wb_in{c}") for c in range(DC)]
        gpre_in = sem("gpre_in")
        small_in = sem("small_in")
        kc_in = sem("kc_in")
        w_scaled = sem("w_scaled")
        ident_done = sem("ident_done")
        x_zeroed = sem("x_zeroed")
        ss_done = sem("ss_done")
        dve_chain = sem("dve_chain")
        h_ready = sem("h_ready")
        fa_full, fa_free = sem("fa_full"), sem("fa_free")
        fg_full, fg_tanh, fg_free = sem("fg_full"), sem("fg_tanh"), sem("fg_free")
        fd_full, fd_free = sem("fd_full"), sem("fd_free")
        fi_full, fi_free = sem("fi_full"), sem("fi_free")
        relu_used = sem("relu_used")
        split_done = sem("split_done")
        kc_split = sem("kc_split")
        kq_out = [sem(f"kq_out{i}") for i in range(2)]
        gst_out = [sem(f"gst_out{i}") for i in range(2)]
        qst_out = [sem(f"qst_out{i}") for i in range(2)]
        u_ready = sem("u_ready")
        win_chain = sem("win_chain")
        d_ready = sem("d_ready")
        np_out = sem("np_out")
        hist_in = sem("hist_in")
        s_ready = sem("s_ready")
        s_out = [sem(f"s_out{i}") for i in range(2)]

        g_stores = [s for s in steps if s[0] in ("GB", "PL")]
        g_slot = {s: i for i, s in enumerate(g_stores)}
        q_slot = {s: i for i, s in enumerate(x for x in steps if x[0] == "Q")}
        tm_order = {s[1]: i for i, s in enumerate(x for x in steps if x[0] == "TM")}
        n_kc = PAST // P

        def width(b):
            return BLOCKS[b][1] * P

        win_end, total = {}, 0
        for s in steps:
            if s[0] == "PL":
                total += s[2] + 1 + (s[1] == 0)
                win_end[s[1:]] = total

        with nc.Block() as block:
            @block.sync
            def _(sp):
                def load_x(i, t):
                    if i >= 3:
                        prev = [u for u in norm_order if norm_order[u] == i - 3][0]
                        sp.wait_ge(fa_full, fa["H", prev, 1] + 1)
                    if t == ST:
                        sp.wait_ge(x_zeroed, 1)
                        sp.dma_start(xs[0:DEC, i % 3, :], A["x_sample"][0]).then_inc(x_in[i % 3], 16)
                    else:
                        sp.dma_start(xs[:, i % 3, :], A["x_prompt"][0, t * P:(t + 1) * P, :]).then_inc(x_in[i % 3], 16)

                order = sorted(norm_order, key=norm_order.get)
                for i in range(3):
                    load_x(i, order[i])
                sp.dma_start(gpre[:], A["g_pre"]).then_inc(gpre_in, 16)
                w_rows = A["w_in"][0].rearrange("(c p) n -> c p n", p=P)
                for c in range(DC):
                    sp.dma_start(W[:, c, C_K:COLS], w_rows[c, :, C_K:COLS]).then_inc(wa_in[c], 16)
                for c in range(DC):
                    sp.dma_start(W[:, c, 0:C_K], w_rows[c, :, 0:C_K]).then_inc(wb_in[c], 16)
                sp.dma_start(pscale[:], A["pool_scale"]).then_inc(small_in, 16)
                sp.dma_start(wpool[:], A["w_pool"][0].rearrange("g c d -> c g d")).then_inc(small_in, 16)
                sp.dma_start(fix[:], A["pool_fix"]).then_inc(small_in, 16)
                sp.dma_start(kc[:], A["cache_kidx"][0, 0].rearrange("(j p) d -> p j d", p=P)).then_inc(kc_in, 16)
                loaded = 3
                n_tm = {0: 0, 1: 0}
                for s in steps:
                    if s[0] == "H":
                        if loaded < NT:
                            load_x(loaded, order[loaded])
                            loaded += 1
                    elif s[0] == "TM":
                        t = s[1]
                        i = tm_order[t] % 2
                        sp.wait_ge(fa_free, fa["TM", t, 1] + 1)
                        new = "prompt" if t < NPT else "sample"
                        a, b, r = (t * P, t * P + P, P) if t < NPT else (0, DEC, DEC)
                        kk = A[f"new_k_{new}"][0, 0, a:b].rearrange("t k d -> t (k d)")
                        vv = A[f"new_v_{new}"][0, 0, a:b].rearrange("t k d -> t (k d)")
                        sp.dma_start(kk, kq[0:r, i, 0:128]).then_inc(kq_out[i], 16)
                        sp.dma_start(vv, kq[0:r, i, 128:256]).then_inc(kq_out[i], 16)
                        sp.dma_start(A[f"new_kidx_{new}"][0, 0, a:b], kq[0:r, i, 512:544]).then_inc(kq_out[i], 16)
                    elif s[0] in ("GB", "PL"):
                        n = g_slot[s]
                        if s[0] == "GB":
                            sp.wait_ge(fg_free, fg[s] + 1)
                            b, g = s[1:]
                            a = BLOCKS[b][0] * P
                            dst = gb_dram[:, g, a:a + width(b)]
                            src = gst[:, n % 2, 0:width(b)]
                        else:
                            sp.wait_ge(fd_free, fd[s] + 1)
                            b, g = s[1:]
                            a = BLOCKS[b][0] * P
                            dst = ma_dram[:, g, a:a + width(b)]
                            src = gst[:, n % 2, 0:width(b)]
                        sp.dma_start(dst, src).then_inc(gst_out[n % 2], 16)
                    elif s[0] == "Q":
                        n = q_slot[s]
                        b, j = s[1:]
                        a = BLOCKS[b][0] * P
                        sp.wait_ge(fa_free, fa[s] + 1)
                        sp.dma_start(q_dram[:, j, a:a + width(b)], qst[:, n % 2, 0:width(b)])\
                          .then_inc(qst_out[n % 2], 16)
                    elif s[0] == "NP":
                        b = s[1]
                        k = b - (len(BLOCKS) - 2)
                        sp.wait_ge(fd_free, fd[s] + 1)
                        sp.dma_start(A["new_pool_prompt" if k == 0 else "new_pool_sample"][0, 0], rows[:])\
                          .then_inc(np_out, 16)
                        if k == 0:
                            sp.wait_ge(np_out, 16)
                            sp.dma_start(rows[:], A["state_pool"][0, 0]).then_inc(hist_in, 16)
                    elif s[0] == "I" and s[2] == NIH - 1 and s[3] == len(score_chunks(s[1])) - 1:
                        t = s[1]
                        n = key_tiles(t) * P
                        sp.wait_ge(s_ready, t + 1)
                        sp.dma_start(s_dram[t, :, 0:n], S[:, t % 2, 0:n]).then_inc(s_out[t % 2], 16)
                for i in range(2):
                    sp.wait_ge(kq_out[i], 48 * len(range(i, NT, 2)))
                    sp.wait_ge(gst_out[i], 16 * len(range(i, len(g_stores), 2)))
                    sp.wait_ge(qst_out[i], 16 * len(range(i, len(q_slot), 2)))
                    sp.wait_ge(s_out[i], 16 * len(range(i, NT, 2)))
                sp.wait_ge(np_out, 32)

            @block.gpsimd
            def _(pool):
                pool.memset(identf[:], 0.0).then_inc(ident_done, 1)
                pool.memset(identb[:], 0.0).then_inc(ident_done, 1)
                pool.memset(onesb[:], 1.0).then_inc(ident_done, 1)
                pool.memset(U[:, :, 0:UOFF], 0.0).then_inc(ident_done, 1)
                pool.wait_ge(ident_done, 4)
                for m in (identf, identb):
                    pool.affine_select(out=m[:], in_=m[:], compare_op=ALU.not_equal, fill=1.0, base=0,
                                       pattern=[[-1, P]], channel_multiplier=1).then_inc(ident_done, 1)
                chain = 0
                for s in steps:
                    if s[0] == "N" and s[1] == ST:
                        i = norm_order[ST]
                        prev = [u for u in norm_order if norm_order[u] == i - 3][0]
                        pool.wait_ge(fa_full, fa["H", prev, 1] + 1)
                        pool.memset(xs[:, i % 3, :], 0.0).then_inc(x_zeroed, 1)
                    elif s[0] == "PL":
                        b, g = s[1:]
                        w = 2 << g
                        T = width(b)
                        k = pool_order[b, g]
                        pool.wait_ge(fa_free, fa["U", b, g] + 1)
                        if b == len(BLOCKS) - 1:
                            pool.wait_ge(fd_free, fd["HIST",] + 1)
                        if k >= 1:
                            prev = [u for u in pool_order if pool_order[u] == k - 1][0]
                            pool.wait_ge(fd_full, fd["PL", *prev] + 1)
                        src = U[:, g, :]
                        step, level = 1, 0
                        while step < w:
                            a = UOFF - (w - 2 * step)
                            dst = win[:, level % 2, :]
                            if level:
                                pool.wait_ge(win_chain, chain)
                            pool.tensor_tensor(dst[:, a:UOFF + T], src[:, a:UOFF + T],
                                               src[:, a - step:UOFF + T - step], ALU.add).then_inc(win_chain, 1)
                            chain += 1
                            src = dst
                            step *= 2
                            level += 1
                        if b == 0:
                            pool.wait_ge(win_chain, chain)
                            pool.tensor_tensor(src[:, UOFF:UOFF + HIST], src[:, UOFF:UOFF + HIST],
                                               fix[:, g, 0:HIST], ALU.mult).then_inc(win_chain, 1)
                            chain += 1
                        if b < len(BLOCKS) - 2:
                            pool.wait_ge(d_ready, k + 1)
                            pool.tensor_copy(U[:, g, 1:UOFF], U[:, g, T + 1:T + UOFF]).then_inc(u_ready, 1)

            @block.scalar
            def _(act):
                for s in steps:
                    if s[0] == "N":
                        t = s[1]
                        i = norm_order[t]
                        act.wait_ge(x_in[i % 3], 16 * (i // 3 + 1))
                        if i:
                            act.wait_ge(ss_done, i)
                        act.activation(junk[:], xs[:, i % 3, :], ACT.Square, accum_out=ss[:, t:t + 1])\
                           .then_inc(ss_done, 1)
                    elif s[0] == "H":
                        t = s[1]
                        for half in range(2):
                            k = fa["H", t, half]
                            act.wait_ge(fa_full, k + 1)
                            tt = (t % 4) * P
                            act.activation(hT[:, 4 * half:4 * half + 4, tt:tt + P],
                                           banks[k % 2][:].rearrange("p (c n) -> p c n", c=4), ACT.Copy)\
                               .then_inc(fa_free, 1)
                    elif s[0] == "TM":
                        t = s[1]
                        o = tm_order[t]
                        for part, (a, b) in enumerate(((0, 256), (256, 552))):
                            k = fa["TM", t, part]
                            act.wait_ge(fa_full, k + 1)
                            if part == 0 and o >= 2:
                                act.wait_ge(kq_out[o % 2], 48 * (o // 2))
                                act.wait_ge(split_done, 5 * (o - 1))
                                act.wait_ge(fd_full, fd["TR", o - 2, 0] + 1)
                            act.activation(kq[:, o % 2, a:b], banks[k % 2][:, 0:b - a], ACT.Copy)\
                               .then_inc(fa_free, 1)
                    elif s[0] == "Q":
                        k, n, T = fa[s], q_slot[s], width(s[1])
                        act.wait_ge(fa_full, k + 1)
                        if n >= 2:
                            act.wait_ge(qst_out[n % 2], 16 * (n // 2))
                        act.activation(qst[:, n % 2, 0:T], banks[k % 2][:, 0:T], ACT.Copy, scale=ATTN_SCALE)\
                           .then_inc(fa_free, 1)
                    elif s[0] == "U":
                        b, g = s[1:]
                        k, T = fa[s], width(b)
                        act.wait_ge(fa_full, k + 1)
                        if 1 <= b < len(BLOCKS) - 1:
                            act.wait_ge(u_ready, pool_order[b - 1, g] + 1)
                        if b == len(BLOCKS) - 1:
                            act.wait_ge(fd_full, fd["NP", b - 1] + 1)
                            act.wait_ge(d_ready, pool_order[b - 1, g] + 1)
                        act.activation(U[:, g, UOFF:UOFF + T], banks[k % 2][:, 0:T], ACT.Copy).then_inc(fa_free, 1)
                    elif s[0] in ("GB", "GA"):
                        k = fg[s]
                        T = width(s[1])
                        act.wait_ge(fg_full, k + 1)
                        if s[0] == "GB":
                            m = g_slot[s]
                            dst = gst[:, m % 2, 0:T]
                            if m >= 2:
                                act.wait_ge(gst_out[m % 2], 16 * (m // 2))
                        else:
                            m = pool_order[s[1:]]
                            dst = sga[:, m % 2, 0:T]
                            if m >= 2:
                                prev = [u for u in pool_order if pool_order[u] == m - 2][0]
                                act.wait_ge(fd_free, fd["PL", *prev] + 1)
                        act.activation(dst, banks[2][:, 0:T], ACT.Tanh, scale=0.5).then_inc(fg_tanh, 1)
                    elif s[0] == "I":
                        k = fi[s]
                        a, b = score_chunks(s[1])[s[3]]
                        act.wait_ge(fi_full, k + 1)
                        if k >= 2:
                            act.wait_ge(relu_used, k - 1)
                        act.activation(relu[:, k % 2, 0:b - a], wide[k % 2][:, 0:b - a], ACT.Relu)\
                           .then_inc(fi_free, 1)

            @block.tensor
            def _(pe):
                def fa_bank(key):
                    k = fa[key]
                    if k >= 2:
                        pe.wait_ge(fa_free, k - 1)
                    return banks[k % 2]

                def fd_bank(key):
                    k = fd[key]
                    if k >= 1:
                        pe.wait_ge(fd_free, k)
                    return banks[3]

                def contract(out, stationary, moving):
                    for c in range(DC):
                        mm = pe.matmul(out, stationary(c), moving(c), start=(c == 0), stop=(c == DC - 1))
                    return mm

                pe.wait_ge(ident_done, 6)
                for s in steps:
                    if s[0] == "H":
                        t = s[1]
                        i = norm_order[t]
                        pe.wait_ge(h_ready, i + 1)
                        for half in range(2):
                            bank = fa_bank(("H", t, half))
                            for c in range(4):
                                col = (4 * half + c) * P
                                tr = pe.transpose(bank[:, c * P:(c + 1) * P], xs[:, i % 3, col:col + P], identf[:])
                            tr.then_inc(fa_full, 1)
                        last_h = fa["H", t, 1]
                    elif s[0] == "TM":
                        t = s[1]
                        tt = (t % 4) * P
                        pe.wait_ge(w_scaled, DC)
                        for part, (a, b) in enumerate(((C_K, C_QI), (C_QI, C_GB))):
                            bank = fa_bank(("TM", t, part))
                            pe.wait_ge(fa_free, last_h + 1)
                            contract(bank[:, 0:b - a], lambda c: hT[:, c, tt:tt + P], lambda c: W[:, c, a:b])\
                                .then_inc(fa_full, 1)
                    elif s[0] in ("Q", "GA", "U", "GB"):
                        b, g = s[1:]
                        T = width(b)
                        if s[0] != "GB":
                            pe.wait_ge(w_scaled, 2 * DC)
                        if s[0] in ("GA", "GB"):
                            k = fg[s]
                            if k:
                                pe.wait_ge(fg_free, k)
                            bank, full = banks[2], fg_full
                        else:
                            bank, full = fa_bank(s), fa_full
                        base = {"Q": C_Q, "GA": C_GA, "U": C_U, "GB": C_GB}[s[0]] + g * P
                        contract(bank[:, 0:T], lambda c: W[:, c, base:base + P], lambda c: hT[:, c, 0:T]).then_inc(full, 1)
                    elif s[0] == "TR":
                        t = s[1]
                        o = tm_order[t]
                        bank = fd_bank(("TR", t, 0))
                        pe.wait_ge(split_done, 5 * (o + 1))
                        pe.transpose(bank[:, 0:P], kq[:, o % 2, 0:P], identf[:])
                        pe.transpose(bank[0:3 * DI, P:2 * P], ks[:], identf[:]).then_inc(fd_full, 1)
                        for half in range(2):
                            bank = fd_bank(("TR", t, 1 + half))
                            for h in range(4):
                                tr = pe.transpose(bank[0:3 * DI, h * P:(h + 1) * P], qs[:, 4 * half + h, :],
                                                  identf[:])
                            tr.then_inc(fd_full, 1)
                    elif s[0] == "KC":
                        j = s[1]
                        bank = fd_bank(s)
                        pe.wait_ge(kc_split, 3 * (j + 1))
                        pe.transpose(bank[0:3 * DI, 0:P], ks[:], identf[:]).then_inc(fd_full, 1)
                    elif s[0] == "HIST":
                        bank = fd_bank(s)
                        pe.wait_ge(hist_in, 16)
                        for g in range(NG):
                            tr = pe.transpose(bank[:, g * 16:g * 16 + HIST], rows[:, g * P:(g + 1) * P],
                                              identf[0:HIST, 0:HIST])
                        tr.then_inc(fd_full, 1)
                    elif s[0] == "NP":
                        b = s[1]
                        bank = fd_bank(s)
                        last = UOFF + (512 if b < len(BLOCKS) - 1 else DEC)
                        for g in range(NG):
                            pe.wait_ge(fa_free, fa["U", b, g] + 1)
                            tr = pe.transpose(bank[0:HIST, g * P:(g + 1) * P], U[:, g, last - HIST:last], identf[:])
                        tr.then_inc(fd_full, 1)
                    elif s[0] == "PL":
                        b, g = s[1:]
                        T = width(b)
                        bank = fd_bank(s)
                        pe.wait_ge(small_in, 48)
                        pe.wait_ge(d_ready, pool_order[b, g] + 1)
                        fin = win[:, g % 2, UOFF:UOFF + T]
                        pe.matmul(bank[:, 0:T], wpool[:, g, :], fin, start=True, stop=True).then_inc(fd_full, 1)
                    elif s[0] == "I":
                        _, t, h, c = s
                        k = fi[s]
                        a, b = score_chunks(t)[c]
                        if k >= 2:
                            pe.wait_ge(fi_free, k - 1)
                        pe.wait_ge(fd_free, fd["TR", t, 2] + 1)
                        for x in range(a, b, 512):
                            y = min(x + 512, b)
                            mm = pe.matmul(wide[k % 2][:, x - a:y - a], qiT[:, t % 2, h, :], kiT[:, x:y],
                                           start=True, stop=True)
                        mm.then_inc(fi_full, 1)

            @block.vector
            def _(dve):
                n = 0
                splits = 0
                scaled = 0

                def scale_w(sems, a, b):
                    dve.wait_ge(gpre_in, 16)
                    for c in range(DC):
                        dve.wait_ge(sems[c], 16)
                        dve.tensor_scalar(W[:, c, a:b], W[:, c, a:b], gpre[:, c:c + 1], None, ALU.mult)\
                           .then_inc(w_scaled, 1)

                for s in steps:
                    if s[0] == "N":
                        t = s[1]
                        i = norm_order[t]
                        dve.wait_ge(ss_done, i + 1)
                        n = inverse_root(dve, dve_chain, n, small[:, 0:1], small[:, 1:2], small[:, 2:3],
                                         ss[:, t:t + 1], 1.0 / D)
                        dve.tensor_scalar(xs[:, i % 3, :], xs[:, i % 3, :], small[:, 1:2], None, ALU.mult)\
                           .then_inc(h_ready, 1)
                        if scaled == 0 and i == 2:
                            scale_w(wa_in, C_K, COLS)
                            scaled = 1
                    elif s[0] == "TM":
                        if scaled == 1:
                            scale_w(wb_in, 0, C_K)
                            dve.wait_ge(small_in, 48)
                            dve.tensor_scalar(pscale[:], pscale[:], 0.5, None, ALU.mult).then_inc(w_scaled, 1)
                            scaled = 2
                        t = s[1]
                        o = tm_order[t]
                        dve.wait_ge(fa_free, fa["TM", t, 1] + 1)
                        if o >= 1:
                            dve.wait_ge(fd_full, fd["TR", o - 1, 2] + 1)
                        if t == ST:
                            dve.wait_ge(fd_full, fd["KC", n_kc - 1] + 1)
                        qi = kq[:, o % 2, 256:512].rearrange("p (h d) -> p h d", h=NIH)
                        ki = kq[:, o % 2, 512:544]
                        dve.tensor_copy(qs[:, :, 0:DI].bitcast(F32R), qi).then_inc(dve_chain, 1)
                        dve.tensor_copy(qs[:, :, DI:2 * DI].bitcast(F32R), qi).then_inc(split_done, 1)
                        dve.tensor_copy(ks[:, 0:DI].bitcast(F32R), ki).then_inc(dve_chain, 1)
                        dve.tensor_copy(ks[:, 2 * DI:3 * DI].bitcast(F32R), ki).then_inc(split_done, 1)
                        if o >= 2:
                            dve.wait_ge(s_ready, o - 1)
                        dve.tensor_scalar(wi[:, o % 2, :], kq[:, o % 2, 544:552], INDEX_SCALE, None, ALU.mult)\
                           .then_inc(split_done, 1)
                        n += 2
                        dve.wait_ge(dve_chain, n)
                        dve.tensor_tensor(qs[:, :, 2 * DI:3 * DI], qi, qs[:, :, 0:DI], ALU.subtract)\
                           .then_inc(split_done, 1)
                        dve.tensor_tensor(ks[:, DI:2 * DI], ki, ks[:, 0:DI], ALU.subtract).then_inc(split_done, 1)
                    elif s[0] == "KC":
                        j = s[1]
                        dve.wait_ge(kc_in, 16)
                        if j == 0:
                            dve.wait_ge(fd_full, fd["TR", NPT - 1, 2] + 1)
                        else:
                            dve.wait_ge(fd_full, fd["KC", j - 1] + 1)
                        dve.tensor_copy(ks[:, 0:DI].bitcast(F32R), kc[:, j, :]).then_inc(kc_split, 1)
                        dve.tensor_copy(ks[:, 2 * DI:3 * DI].bitcast(F32R), kc[:, j, :]).then_inc(kc_split, 1)
                        dve.wait_ge(kc_split, 3 * j + 2)
                        dve.tensor_tensor(ks[:, DI:2 * DI], kc[:, j, :], ks[:, 0:DI], ALU.subtract)\
                           .then_inc(kc_split, 1)
                        if j == 0:
                            last = ("I", NPT - 1, NIH - 1, len(score_chunks(NPT - 1)) - 1)
                            dve.wait_ge(fi_full, fi[last] + 1)
                        dve.wait_ge(fd_full, fd[s] + 1)
                        dve.tensor_copy(kiT[:, j * P:(j + 1) * P], banks[3][0:3 * DI, 0:P]).then_inc(fd_free, 1)
                    elif s[0] == "HIST":
                        dve.wait_ge(fd_full, fd[s] + 1)
                        dve.wait_ge(d_ready, pool_order[len(BLOCKS) - 2, NG - 1] + 1)
                        dve.tensor_copy(U[:, :, 1:UOFF], banks[3][:, 0:64].rearrange("p (g r) -> p g r", g=NG)
                                        [:, :, 0:HIST]).then_inc(fd_free, 1)
                    elif s[0] == "NP":
                        dve.wait_ge(fd_full, fd[s] + 1)
                        dve.tensor_copy(rows[:], banks[3][0:HIST, :]).then_inc(fd_free, 1)
                    elif s[0] in ("GB", "GA"):
                        k = fg[s]
                        T = width(s[1])
                        dve.wait_ge(fg_tanh, k + 1)
                        if s[0] == "GB":
                            dst = gst[:, g_slot[s] % 2, 0:T]
                        else:
                            dst = sga[:, s[2] % 2, 0:T]
                        dve.scalar_tensor_tensor(dst, dst, 1.0, banks[2][:, 0:T], ALU.add, ALU.mult)\
                           .then_inc(fg_free, 1)
                    elif s[0] == "TR":
                        t = s[1]
                        o = tm_order[t]
                        k = fd["TR", t, 0]
                        dve.wait_ge(fd_full, k + 1)
                        if t < NPT:
                            dve.tensor_copy(kT[:, t * P:(t + 1) * P], banks[3][:, 0:P]).then_inc(dve_chain, 1)
                            n += 1
                        at = place_of(t) * P
                        dve.tensor_copy(kiT[:, at:at + P], banks[3][0:3 * DI, P:2 * P]).then_inc(fd_free, 1)
                        for half in range(2):
                            dve.wait_ge(fd_full, k + 2 + half)
                            dve.tensor_copy(qiT[:, t % 2, 4 * half:4 * half + 4, :],
                                            banks[3][0:3 * DI, :].rearrange("p (h n) -> p h n", h=4))\
                               .then_inc(fd_free, 1)
                    elif s[0] == "PD":
                        b, g = s[1:]
                        T = width(b)
                        dve.wait_ge(win_chain, win_end[b, g])
                        fin = win[:, g % 2, UOFF:UOFF + T]
                        dve.scalar_tensor_tensor(fin, fin, 1.0 / (2 << g), U[:, g, UOFF:UOFF + T], ALU.mult,
                                                 ALU.subtract).then_inc(d_ready, 1)
                    elif s[0] == "PL":
                        b, g = s[1:]
                        T = width(b)
                        m = g_slot[s]
                        if m >= 2:
                            dve.wait_ge(gst_out[m % 2], 16 * (m // 2))
                        dve.wait_ge(fd_full, fd[s] + 1)
                        dve.wait_ge(fg_free, fg["GA", b, g] + 1)
                        dve.wait_ge(w_scaled, 2 * DC + 1)
                        dve.scalar_tensor_tensor(gst[:, m % 2, 0:T], banks[3][:, 0:T], pscale[:, g:g + 1],
                                                 sga[:, g % 2, 0:T], ALU.mult, ALU.mult).then_inc(fd_free, 1)
                    elif s[0] == "I":
                        _, t, h, c = s
                        k = fi[s]
                        a, b = score_chunks(t)[c]
                        dve.wait_ge(fi_free, k + 1)
                        if h == 0 and t >= 2:
                            dve.wait_ge(s_out[t % 2], 16 * (t // 2))
                        w = wi[:, t % 2, h:h + 1]
                        if h == 0:
                            dve.tensor_scalar(S[:, t % 2, a:b], relu[:, k % 2, 0:b - a], w, None, ALU.mult)\
                               .then_inc(relu_used, 1)
                        else:
                            dve.wait_ge(relu_used, fi["I", t, h - 1, c] + 1)
                            dve.scalar_tensor_tensor(S[:, t % 2, a:b], relu[:, k % 2, 0:b - a], w,
                                                     S[:, t % 2, a:b], ALU.mult, ALU.add).then_inc(relu_used, 1)
                        if h == NIH - 1 and c == len(score_chunks(t)) - 1:
                            nk = key_tiles(t) * P
                            dve.wait_ge(relu_used, k + 1)
                            dve.tensor_reduce(small[:, 0:1], S[:, t % 2, 0:nk], AX.X, ALU.min)\
                               .then_inc(dve_chain, 1)
                            dve.tensor_reduce(small[:, 1:2], S[:, t % 2, 0:nk], AX.X, ALU.max)\
                               .then_inc(dve_chain, 1)
                            n += 2
                            dve.wait_ge(dve_chain, n)
                            dve.scalar_tensor_tensor(small[:, 2:3], small[:, 0:1], -1.0, small[:, 1:2], ALU.mult,
                                                     ALU.max).then_inc(dve_chain, 1)
                            n += 1
                            dve.wait_ge(dve_chain, n)
                            dve.tensor_scalar(top[:, t:t + 1], small[:, 2:3], 1e-20, None, ALU.max)\
                               .then_inc(dve_chain, 1)
                            dve.tensor_scalar(small[:, 3:4], small[:, 2:3], 1e-20, UNSEEN, ALU.max, ALU.mult)\
                               .then_inc(dve_chain, 1)
                            n += 2
                            dve.wait_ge(dve_chain, n)
                            blind, a = (slice(0, CHUNK), nk - CHUNK) if t < NPT else (slice(0, P), PAST + DEC)
                            dve.tensor_scalar(S[blind, t % 2, a:nk], S[blind, t % 2, a:nk], 0.0, small[blind, 3:4],
                                              ALU.mult, ALU.add).then_inc(s_ready, 1)


def phase2(nc, A, sb, sem, identf, identb, onesb, kT, top, banks, wide, q_dram, gb_dram, ma_dram, s_dram,
           g_dram, k_dram):
    groups = [(t, t + 1) for t in range(0, NPT, 2)] + [(ST,)]
    NGR = len(groups)

    def group(p):
        return groups[p] if 0 <= p < NGR else ()

    def chunks(t):
        n = key_tiles(t) * P
        return [(a, min(a + 512, n)) for a in range(0, n, 512)]

    def near(t, kt):
        return place_of(t) - kt < BIAS_TILES

    fx, fl, near_count = {}, {}, {}
    n_near = 0
    for t in range(NT):
        for h in range(NH):
            for c in range(len(chunks(t))):
                fx[t, h, c] = len(fx)
        for kv in range(NKV):
            for kt in range(key_tiles(t)):
                fl[t, kv, kt] = len(fl)
                n_near += near(t, kt)
                near_count[t, kv, kt] = n_near

    def jobs(p):
        return [(t, kv, kt) for t in group(p) for kv in range(NKV) for kt in range(key_tiles(t))]

    def last_fl(t, kv=NKV - 1):
        return fl[t, kv, key_tiles(t) - 1]

    def last_fx(t):
        return fx[t, NH - 1, len(chunks(t)) - 1]

    sample_keys = ((banks[2], 0, 4), (banks[3], 4, 8), (wide[1], 8, 9))
    NSK = PAST // P + 1

    def searched(p):
        return len(group(p)) > 0 and group(p)[0] >= TOPK // P

    with ExitStack() as st:
        k2 = [sb(st, f"k2_{kv}", [P, SEQ], F32R) for kv in range(NKV)]
        vx = sb(st, "vx", [P, NPT, 3, HD], F32)
        EB = sb(st, "EB", [P, NH, BIAS_W], F32)
        relb = sb(st, "relb", [NBUCKETS, NH], F32)
        nfar = sb(st, "nfar", [NH, 1], F32)
        wout = sb(st, "wout", [P, DC, D], F32)
        gpost = sb(st, "gpost", [P, D], F32)
        S = sb(st, "S2", [P, 2, SEQ], F32)
        near_s = sb(st, "near_s", [P, 2, SEQ], F16)
        mask = sb(st, "mask", [P, 2, SEQ], BF16)
        above = sb(st, "above", [P, SEQ], BF16)
        reach = sb(st, "reach", [P, SEQ], BF16)
        cum = sb(st, "cum", [P, SEQ], F32)
        junk = above
        q = sb(st, "q", [P, NKV, GRP, P], F32)
        qh = sb(st, "qh", [P, 2, NKV, GRP, P], F32R)
        ql = sb(st, "ql", [P, 2, NKV, GRP, P], F32R)
        gb = sb(st, "gb", [P, 2, 512], F32)
        ma = sb(st, "ma", [P, 2, NG, P], F32)
        xr = sb(st, "xr", [P, 2, D], F32)
        E = sb(st, "E", [P, 4, GRP, P], F32)
        shift = sb(st, "shift", [P, 2, NH, P], BF16)
        osum = sb(st, "osum", [P, 2, 512], F32)
        den = sb(st, "den", [P, 2, 512], F32)
        yT = sb(st, "yT", [P, 2, 4, P], F32)
        sq = sb(st, "sq", [P, 512], BF16)
        unit, scale, centre, cand, cnt, side, room, lo, hi = (sb(st, f"search{i}", [P, 2], F32) for i in range(9))
        width = sb(st, "width", [P, 1], F32)
        mxp = sb(st, "mxp", [P, NH, 4], F32)
        nmax = sb(st, "nmax", [P, NH], F32)
        ss2 = sb(st, "ss2", [P, NT, 2], F32)
        root = sb(st, "root", [P, 4, 2], F32)
        klow = kT[:].bitcast(F32R)
        osb = kT[:].rearrange("p (a n) -> p a n", a=2)
        flat = wout[:].rearrange("p c n -> p (c n)")
        ks_high = flat[:, 0:NSK * P].bitcast(F32R)
        ks_low = flat[:, NSK * P:2 * NSK * P].bitcast(F32R)
        ck = S[:, 1, 0:NSK * P].rearrange("p (j n) -> p j n", n=NKV * HD)
        onehot = cum[0:NBUCKETS, 0:GLEN]
        G = cum[0:NH, GLEN:2 * GLEN]

        bias_in, bias_out = sem("bias_in"), sem("bias_out")
        eb_in = sem("eb_in")
        ck_in, ck_zeroed = sem("ck_in"), sem("ck_zeroed")
        wout_in = sem("wout_in")
        S_in = [sem(f"S_in{i}") for i in range(2)]
        S_used = sem("S_used")
        q_in, q_split = sem("q_in"), sem("q_split")
        v_in = sem("v_in")
        k_split, k_low, k_moved = sem("k_split"), sem("k_low"), sem("k_moved")
        ks_split, ks_lowered, ks_out, ks_in = sem("ks_split"), sem("ks_lowered"), sem("ks_out"), sem("ks_in")
        gb_in = [sem(f"gb_in{i}") for i in range(2)]
        ma_in = [sem(f"ma_in{i}") for i in range(2)]
        xr_in = [sem(f"xr_in{i}") for i in range(2)]
        y_out = [sem(f"y_out{i}") for i in range(2)]
        g_full, nfar_done, g_exp = sem("g_full"), sem("nfar_done"), sem("g_exp")
        ckt_full = sem("ckt_full")
        dk = sem("dk")
        mask_done = sem("mask_done")
        plain_mask = sem("plain_mask")
        fx_full, fx_free = sem("fx_full"), sem("fx_free")
        shift_done = sem("shift_done")
        fl_full, fl_free = sem("fl_full"), sem("fl_free")
        biased = sem("biased")
        pv_step = sem("pv_step")
        sums_out, recip_done = sem("sums_out"), sem("recip_done")
        mean_done, yT_done = sem("mean_done"), sem("yT_done")
        o_full, o_free = sem("o_full"), sem("o_free")
        post_done = sem("post_done")
        res_done = sem("res_done")

        with nc.Block() as block:
            @block.sync
            def _(sp):
                def load_S(p):
                    if not searched(p):
                        return
                    if p >= 2:
                        sp.wait_ge(S_used, 2 * (p - 1))
                    for i, t in enumerate(group(p)):
                        if p == 1 and i == 1:
                            sp.wait_ge(ckt_full, 3)
                        n = key_tiles(t) * P
                        sp.dma_start(S[:, i, 0:n], s_dram[t, :, 0:n]).then_inc(S_in[i], 16)

                def load_q(t):
                    if t >= NT:
                        return
                    if t >= 1:
                        sp.wait_ge(q_split, 2 * t)
                    for kv in range(NKV):
                        for half in range(2):
                            sp.dma_start(q[half * HD:(half + 1) * HD, kv],
                                         q_dram[kv * HD:(kv + 1) * HD, :, t * P:(t + 1) * P]).then_inc(q_in, 16)

                sp.dma_start(onehot, A["bucket_onehot"]).then_inc(bias_in, 16)
                sp.dma_start(relb[:], A["rel_bias"]).then_inc(bias_in, 16)
                load_q(0)
                sp.wait_ge(ck_zeroed, 2)
                sp.dma_start(ck[:, 0:PAST // P, :], A["cache_k"][0, 0].rearrange("(j p) k d -> p j (k d)", p=P))\
                  .then_inc(ck_in, 16)
                sp.dma_start(ck[0:DEC, PAST // P, :], A["new_k_sample"][0, 0].rearrange("t k d -> t (k d)"))\
                  .then_inc(ck_in, 16)
                for kv in range(NKV):
                    sp.dma_start(vx[:, :, 2 * kv, :],
                                 A["new_v_prompt"][0, 0, :, kv].rearrange("(j p) d -> p j d", p=P)).then_inc(v_in, 16)
                sp.wait_ge(k_low, 2)
                sp.dma_start(k2[0][HD:P, :].bitcast(F32), klow[0:HD, :].bitcast(F32)).then_inc(k_moved, 16)
                sp.dma_start(k2[1][0:HD, :].bitcast(F32), klow[HD:P, :].bitcast(F32)).then_inc(k_moved, 16)
                sp.wait_ge(g_exp, 2)
                sp.dma_start(g_dram, G.rearrange("h (a n) -> h a n", a=1).broadcast_to([NH, P, GLEN]))\
                  .then_inc(bias_out, 16)
                load_q(1)
                load_S(1)
                sp.wait_ge(bias_out, 16)
                sp.dma_start(EB[:], bass.AP(g_dram.tensor, P - 1, [[GLEN - 1, P], [P * GLEN, NH], [1, BIAS_W]]))\
                  .then_inc(eb_in, 16)
                sp.wait_ge(ks_lowered, 3)
                for part, swap in ((ks_high, 0), (ks_low, 1)):
                    for kv in range(NKV):
                        at = (kv ^ swap) * HD
                        sp.dma_start(k_dram[kv, at:at + HD, :], part[kv * HD:(kv + 1) * HD, :].bitcast(F32))\
                          .then_inc(ks_out, 16)
                sp.wait_ge(ks_out, 64)
                sp.dma_start(wout[:], A["w_out"][0].rearrange("(c p) n -> p c n", p=P)).then_inc(wout_in, 16)
                sp.dma_start(gpost[:], A["g_post"].broadcast_to([P, D])).then_inc(wout_in, 16)

                for p in range(NGR + 2):
                    if p == NGR - 1:
                        sp.wait_ge(pv_step, last_fl(ST - 1) + 1)
                        for kv in range(NKV):
                            sp.dma_start(k2[kv][:, 0:NSK * P].bitcast(F32), k_dram[kv]).then_inc(ks_in, 16)
                            sp.dma_start(vx[:, 0:PAST // P, 2 * kv, :],
                                         A["cache_v"][0, 0, :, kv].rearrange("(j p) d -> p j d", p=P))\
                              .then_inc(ks_in, 16)
                            sp.dma_start(vx[0:DEC, PAST // P, 2 * kv, :], A["new_v_sample"][0, 0, :, kv])\
                              .then_inc(ks_in, 16)
                    if p >= 1:
                        load_S(p + 1)
                    for t in group(p - 2):
                        sp.wait_ge(res_done, t + 1)
                        if t < NPT:
                            sp.dma_start(A["y_prompt"][0, t * P:(t + 1) * P, :], osb[:, t % 2, :])\
                              .then_inc(y_out[t % 2], 16)
                        else:
                            sp.dma_start(A["y_sample"][0], osb[0:DEC, t % 2, :]).then_inc(y_out[t % 2], 16)
                    for t in group(p - 1):
                        if t >= 2:
                            sp.wait_ge(res_done, t - 1)
                        if t < NPT:
                            sp.dma_start(xr[:, t % 2, :], A["x_prompt"][0, t * P:(t + 1) * P, :])\
                              .then_inc(xr_in[t % 2], 16)
                        else:
                            sp.dma_start(xr[0:DEC, t % 2, :], A["x_sample"][0]).then_inc(xr_in[t % 2], 16)
                    for t in group(p):
                        if t >= 2:
                            sp.wait_ge(yT_done, t - 1)
                        sp.dma_start(gb[:, t % 2].rearrange("p (j n) -> p j n", j=GRP),
                                     gb_dram[:, :, t * P:(t + 1) * P]).then_inc(gb_in[t % 2], 16)
                    for t in group(p):
                        if t >= 2:
                            sp.wait_ge(o_full, 2 * (t - 1))
                        sp.dma_start(ma[:, t % 2], ma_dram[:, :, t * P:(t + 1) * P]).then_inc(ma_in[t % 2], 16)
                    for t in group(p + 1):
                        load_q(t)
                for i in range(2):
                    sp.wait_ge(y_out[i], 16 * len(range(i, NT, 2)))

            @block.gpsimd
            def _(pool):
                def low(t):
                    pool.wait_ge(q_split, 2 * t + 1)
                    if t >= 2:
                        pool.wait_ge(fl_full, last_fl(t - 2) + 1)
                    pool.tensor_tensor(ql[:, t % 2], q[:], qh[:, t % 2].bitcast(F32), ALU.subtract)\
                        .then_inc(q_split, 1)

                pool.memset(ck[:, PAST // P, :], 0.0).then_inc(ck_zeroed, 1)
                pool.memset(vx[:], 2.0).then_inc(ck_zeroed, 1)
                for t in range(TOPK // P):
                    n = key_tiles(t) * P
                    pool.memset(mask[:, t, 0:n], 0.0).then_inc(plain_mask, 1)
                    pool.wait_ge(plain_mask, 2 * t + 1)
                    pool.memset(mask[0:CHUNK, t, n - CHUNK:n], MASKED).then_inc(plain_mask, 1)
                low(0)
                low(1)
                pool.wait_ge(eb_in, 16)
                for p in range(NGR + 2):
                    for t in group(p - 2):
                        r = P if t < NPT else DEC
                        pool.wait_ge(xr_in[t % 2], 16 * (t // 2 + 1))
                        pool.wait_ge(post_done, t + 1)
                        pool.tensor_tensor(osb[0:r, t % 2, :], osb[0:r, t % 2, :], xr[0:r, t % 2, :], ALU.add)\
                            .then_inc(res_done, 1)
                    for t in group(p - 1):
                        pool.wait_ge(recip_done, t + 1)
                        pool.tensor_tensor(osum[:, t % 2], osum[:, t % 2], den[:, t % 2], ALU.mult)\
                            .then_inc(mean_done, 1)
                        pool.wait_ge(gb_in[t % 2], 16 * (t // 2 + 1))
                        if t >= 2:
                            pool.wait_ge(o_full, 2 * (t - 1))
                        pool.wait_ge(mean_done, t + 1)
                        pool.tensor_tensor(yT[:, t % 2].rearrange("p j n -> p (j n)"), osum[:, t % 2], gb[:, t % 2],
                                           ALU.mult).then_inc(yT_done, 1)
                    for t, kv, kt in jobs(p):
                        if near(t, kt):
                            k = fl[t, kv, kt]
                            off = (place_of(t) - kt) * P
                            pool.wait_ge(fl_free, k + 1)
                            pool.tensor_tensor(E[:, k % 4], E[:, k % 4],
                                               EB[:, kv * GRP:(kv + 1) * GRP, off:off + P], ALU.mult)\
                                .then_inc(biased, 1)
                        if (kv, kt) == (NKV - 1, key_tiles(t) - 1) and t + 2 < NT:
                            low(t + 2)

            @block.scalar
            def _(act):
                def high(t):
                    act.wait_ge(q_in, 64 * (t + 1))
                    if t >= 2:
                        act.wait_ge(fl_full, last_fl(t - 2) + 1)
                    act.activation(qh[:, t % 2], q[:], ACT.Copy).then_inc(q_split, 1)

                def take_sums(t, kv):
                    act.wait_ge(pv_step, last_fl(t, kv) + 1)
                    if t >= 2:
                        act.wait_ge(yT_done, t - 1)
                    own = slice(kv * HD, (kv + 1) * HD)
                    other = slice((1 - kv) * HD, (2 - kv) * HD)
                    act.activation(osum[own, t % 2], wide[0][own, kv * 512:(kv + 1) * 512], ACT.Copy)\
                       .then_inc(sums_out, 1)
                    act.activation(den[own, t % 2], wide[0][other, kv * 512:(kv + 1) * 512], ACT.Copy)\
                       .then_inc(sums_out, 1)

                act.activation(k2[0][0:HD, :], kT[0:HD, :], ACT.Copy).then_inc(k_split, 1)
                act.activation(k2[1][HD:P, :], kT[HD:P, :], ACT.Copy).then_inc(k_split, 1)
                act.wait_ge(g_full, 1)
                act.wait_ge(nfar_done, 1)
                act.activation(G[:, 0:512], banks[0][0:NH, :], ACT.Exp, bias=nfar[:]).then_inc(g_exp, 1)
                act.activation(G[:, 512:GLEN], banks[1][0:NH, 0:GLEN - 512], ACT.Exp, bias=nfar[:]).then_inc(g_exp, 1)
                high(0)
                for i, (src, a, b) in enumerate(sample_keys):
                    act.wait_ge(ckt_full, i + 1)
                    act.activation(ks_high[:, a * P:b * P], src[:, 0:(b - a) * P], ACT.Copy).then_inc(ks_split, 1)
                high(1)
                for p in range(NGR + 1):
                    for t in group(p - 1):
                        if t == 0:
                            act.wait_ge(k_moved, 32)
                        for i in range(2):
                            act.wait_ge(o_full, 2 * t + i + 1)
                            if 2 * t + i:
                                act.wait_ge(o_free, 4 * t + 2 * i)
                            act.activation(sq[:], wide[1][:, i * 512:(i + 1) * 512], ACT.Square,
                                           accum_out=ss2[:, t, i:i + 1]).then_inc(o_free, 1)
                            if i == 0 and t >= 2:
                                act.wait_ge(y_out[t % 2], 16 * (t // 2))
                            act.activation(osb[:, t % 2, i * 512:(i + 1) * 512], wide[1][:, i * 512:(i + 1) * 512],
                                           ACT.Copy).then_inc(o_free, 1)
                    waiting = []
                    for t, kv, kt in jobs(p):
                        k = fl[t, kv, kt]
                        act.wait_ge(fl_full, k + 1)
                        if k >= 4:
                            act.wait_ge(pv_step, k - 3)
                        act.activation(E[:, k % 4], banks[2 + k % 2][:].rearrange("p (j n) -> p j n", j=GRP),
                                       ACT.Exp).then_inc(fl_free, 1)
                        while waiting and last_fl(*waiting[0]) <= k - 2:
                            take_sums(*waiting.pop(0))
                        if kt == key_tiles(t) - 1:
                            waiting.append((t, kv))
                            if kv == NKV - 1 and t + 2 < NT:
                                high(t + 2)
                    for w in waiting:
                        take_sums(*w)

            @block.tensor
            def _(pe):
                pe.wait_ge(bias_in, 32)
                pe.matmul(banks[0][0:NH, :], relb[:], onehot[:, 0:512], start=True, stop=True)
                pe.matmul(banks[1][0:NH, 0:GLEN - 512], relb[:], onehot[:, 512:GLEN], start=True, stop=True)\
                  .then_inc(g_full, 1)
                pe.wait_ge(ck_in, 32)
                for dst, a, b in sample_keys:
                    for j in range(a, b):
                        tr = pe.transpose(dst[:, (j - a) * P:(j - a + 1) * P], ck[:, j, :], identf[:])
                    tr.then_inc(ckt_full, 1)
                pe.wait_ge(g_exp, 2)
                pe.wait_ge(ks_lowered, 3)
                pe.wait_ge(k_split, 2)
                pe.wait_ge(k_moved, 32)

                def max_logits(t, h, c):
                    if h == 0 and c == 0:
                        pe.wait_ge(q_split, 2 * t + 1)
                        if t == ST:
                            pe.wait_ge(ks_in, 96)
                    k = fx[t, h, c]
                    if k >= 2:
                        pe.wait_ge(fx_free, k - 1)
                    kv, j = divmod(h, GRP)
                    a, b = chunks(t)[c]
                    pe.matmul(banks[k % 2][:, 0:b - a], qh[:, t % 2, kv, j, :], k2[kv][:, a:b], start=True, stop=True)\
                      .then_inc(fx_full, 1)

                def logits(t, kv, kt):
                    k = fl[t, kv, kt]
                    if kv == 0 and kt == 0:
                        pe.wait_ge(q_split, 2 * t + 2)
                        pe.wait_ge(shift_done, t + 1)
                    if k >= 2:
                        pe.wait_ge(fl_free, k - 1)
                    bank = banks[2 + k % 2][:].rearrange("p (j n) -> p j n", j=GRP)
                    keys = k2[kv][:, kt * P:(kt + 1) * P]
                    pe.matmul(bank, keys, qh[:, t % 2, kv], start=True, stop=False)
                    pe.matmul(bank, keys, ql[:, t % 2, kv], start=False, stop=False)
                    pe.matmul(bank, mask[:, t % 2, kt * P:(kt + 1) * P],
                              identb[:].rearrange("p (a n) -> p a n", a=1).broadcast_to([P, GRP, P]),
                              start=False, stop=False)
                    pe.matmul(bank, onesb[:], shift[:, t % 2, kv * GRP:(kv + 1) * GRP], start=False, stop=True)\
                      .then_inc(fl_full, 1)

                def weighted_values(t, kv, kt):
                    k = fl[t, kv, kt]
                    if near(t, kt):
                        pe.wait_ge(biased, near_count[t, kv, kt])
                    else:
                        pe.wait_ge(fl_free, k + 1)
                    if kt == 0 and t >= 1:
                        pe.wait_ge(sums_out, 4 * (t - 1) + 2 * (kv + 1))
                    pe.matmul(wide[0][:, kv * 512:(kv + 1) * 512], vx[:, kt, kv:kv + 2, :].rearrange("p a d -> p (a d)"),
                              E[:, k % 4].rearrange("p j n -> p (j n)"), start=(kt == 0),
                              stop=(kt == key_tiles(t) - 1)).then_inc(pv_step, 1)

                def attention(p):
                    todo = jobs(p)
                    if p == 0:
                        pe.wait_ge(v_in, 32)
                    for i in range(len(todo) + 2):
                        if i < len(todo):
                            logits(*todo[i])
                        if 2 <= i:
                            weighted_values(*todo[i - 2])

                def output(t, i, c):
                    if i == 0 and c == 0:
                        pe.wait_ge(wout_in, 32)
                        pe.wait_ge(ma_in[t % 2], 16 * (t // 2 + 1))
                    if c == 0 and t >= 1:
                        pe.wait_ge(o_free, 4 * (t - 1) + 2 * (i + 1))
                    if c == NG:
                        pe.wait_ge(yT_done, t + 1)
                    stat = ma[:, t % 2, c, :] if c < NG else yT[:, t % 2, c - NG, :]
                    mm = pe.matmul(wide[1][:, i * 512:(i + 1) * 512], stat, wout[:, c, i * 512:(i + 1) * 512],
                                   start=(c == 0), stop=(c == DC - 1))
                    if c == DC - 1:
                        mm.then_inc(o_full, 1)

                for p in range(NGR + 1):
                    outs = [(t, i, c) for t in group(p - 1) for i in range(2) for c in range(DC)]
                    maxs = [(t, h, c) for t in group(p) for h in range(NH) for c in range(len(chunks(t)))]
                    if p >= NGR - 1:
                        for o in outs:
                            output(*o)
                        outs = []
                    for i, x in enumerate(maxs):
                        max_logits(*x)
                        for o in outs[i * len(outs) // len(maxs):(i + 1) * len(outs) // len(maxs)]:
                            output(*o)
                    attention(p)

            @block.vector
            def _(dve):
                n = 0

                def link(ins):
                    nonlocal n
                    ins.then_inc(dk, 1)
                    n += 1

                dve.wait_ge(k_split, 2)
                dve.tensor_tensor(klow[0:HD, :], kT[0:HD, :], k2[0][0:HD, :].bitcast(F32), ALU.subtract)\
                   .then_inc(k_low, 1)
                dve.tensor_tensor(klow[HD:P, :], kT[HD:P, :], k2[1][HD:P, :].bitcast(F32), ALU.subtract)\
                   .then_inc(k_low, 1)
                dve.wait_ge(g_full, 1)
                dve.tensor_scalar(nfar[:], banks[1][0:NH, GLEN - 513:GLEN - 512], -1.0, None, ALU.mult)\
                   .then_inc(nfar_done, 1)
                for i, (src, a, b) in enumerate(sample_keys):
                    dve.wait_ge(ks_split, i + 1)
                    dve.tensor_tensor(ks_low[:, a * P:b * P], src[:, 0:(b - a) * P],
                                      ks_high[:, a * P:b * P].bitcast(F32), ALU.subtract).then_inc(ks_lowered, 1)
                dve.wait_ge(bias_out, 16)

                def search(p, level):
                    nonlocal n
                    tiles = group(p)
                    m = len(tiles)
                    cols = slice(0, m)
                    if level == 0:
                        a, b = tiles[0], tiles[-1] + 1
                        link(dve.memset(centre[:, cols], 0.0))
                        link(dve.tensor_scalar(unit[:, cols], top[:, a:b], 1.0 / SPAN, None, ALU.mult))
                        dve.wait_ge(dk, n)
                        link(dve.reciprocal(scale[:, cols], unit[:, cols]))
                    else:
                        link(dve.tensor_tensor(side[:, cols], cand[:, cols], unit[:, cols], ALU.mult))
                        link(dve.tensor_scalar(scale[:, cols], scale[:, cols], float(ZOOM), None, ALU.mult))
                        dve.wait_ge(dk, n)
                        link(dve.tensor_tensor(centre[:, cols], centre[:, cols], side[:, cols], ALU.add))
                        link(dve.tensor_scalar(unit[:, cols], unit[:, cols], 1.0 / ZOOM, None, ALU.mult))
                    link(dve.memset(cand[:, cols], 0.0))
                    link(dve.memset(width[:], 2.0 * REACH))
                    dve.wait_ge(dk, n)
                    if level > 0:
                        for edge, sign in ((lo, -1), (hi, 1)):
                            link(dve.scalar_tensor_tensor(edge[:, cols], unit[:, cols], sign * 1.5 * REACH,
                                                          centre[:, cols], ALU.mult, ALU.add))
                        dve.wait_ge(dk, n)
                        for i, t in enumerate(tiles):
                            w = key_tiles(t) * P
                            link(dve.tensor_scalar(S[:, i, 0:w], S[:, i, 0:w], lo[:, i:i + 1], hi[:, i:i + 1],
                                                   ALU.max, ALU.min))
                        dve.wait_ge(dk, n)
                    for i, t in enumerate(tiles):
                        w = key_tiles(t) * P
                        if level == 0:
                            dve.wait_ge(S_in[i], 16 * p)
                        ins = dve.tensor_scalar(near_s[:, i, 0:w], S[:, i, 0:w], centre[:, i:i + 1],
                                                scale[:, i:i + 1], ALU.subtract, ALU.mult)
                        if level == len(ROUNDS) - 1:
                            ins.then_inc(S_used, 1)
                        else:
                            link(ins)
                    if level == len(ROUNDS) - 1:
                        dve.wait_ge(S_used, tiles[-1] - TOPK // P + 1)
                    base, each = n, m + 3
                    with dve.Fori(0, ROUNDS[level]) as r:
                        at = r * each + base
                        dve.wait_ge(dk, at)
                        for i, t in enumerate(tiles):
                            w = key_tiles(t) * P
                            dve.tensor_scalar((junk, reach)[i][:, 0:w], near_s[:, i, 0:w], cand[:, i:i + 1], None,
                                              ALU.is_ge, ALU.add, accum_out=cnt[:, i:i + 1]).then_inc(dk, 1)
                        dve.tensor_scalar(width[:], width[:], 0.5, None, ALU.mult).then_inc(dk, 1)
                        dve.wait_ge(dk, at + m)
                        dve.tensor_scalar(side[:, cols], cnt[:, cols], TOPK - 0.5, 0.5, ALU.is_ge, ALU.subtract)\
                           .then_inc(dk, 1)
                        dve.wait_ge(dk, at + m + 2)
                        dve.scalar_tensor_tensor(cand[:, cols], side[:, cols], width[:], cand[:, cols],
                                                 ALU.mult, ALU.add).then_inc(dk, 1)
                    n = base + each * ROUNDS[level]
                    dve.wait_ge(dk, n)

                def ends(p):
                    half = REACH / 2.0 ** ROUNDS[-1]
                    cols = slice(0, len(group(p)))
                    link(dve.tensor_scalar(lo[:, cols], cand[:, cols], half, None, ALU.subtract))
                    link(dve.tensor_scalar(hi[:, cols], cand[:, cols], half, None, ALU.add))
                    dve.wait_ge(dk, n)

                def set_mask(t):
                    nonlocal n
                    i = group_column(t)
                    w = key_tiles(t) * P
                    s = near_s[:, i, 0:w]
                    c = cnt[:, i:i + 1]
                    dve.wait_ge(fl_full, last_fl(t - 2) + 1)
                    if t > TOPK // P:
                        dve.wait_ge(mask_done, t - TOPK // P)
                    link(dve.tensor_scalar(above[:, 0:w], s, hi[:, i:i + 1], None, ALU.is_ge, ALU.add, accum_out=c))
                    link(dve.tensor_scalar(reach[:, 0:w], s, lo[:, i:i + 1], None, ALU.is_ge))
                    dve.wait_ge(dk, n)
                    link(dve.tensor_scalar(room[:, i:i + 1], c, -1.0, float(TOPK), ALU.mult, ALU.add))
                    link(dve.tensor_tensor_scan(cum[:, 0:w], reach[:, 0:w], above[:, 0:w], 0.0, ALU.add,
                                                ALU.subtract))
                    link(dve.tensor_tensor(above[:, 0:w], reach[:, 0:w], above[:, 0:w], ALU.add))
                    dve.wait_ge(dk, n)
                    link(dve.scalar_tensor_tensor(reach[:, 0:w], cum[:, 0:w], room[:, i:i + 1], above[:, 0:w],
                                                  ALU.is_gt, ALU.is_ge))
                    dve.wait_ge(dk, n)
                    dve.tensor_scalar(mask[:, t % 2, 0:w], reach[:, 0:w], MASKED, None, ALU.mult)\
                       .then_inc(mask_done, 1)

                def group_column(t):
                    return t % 2

                def maxima(t):
                    nonlocal n
                    if t < TOPK // P:
                        dve.wait_ge(plain_mask, 2 * (t + 1))
                    else:
                        dve.wait_ge(mask_done, t + 1 - TOPK // P)
                    nc_ = len(chunks(t))
                    for h in range(NH):
                        for c, (a, b) in enumerate(chunks(t)):
                            k = fx[t, h, c]
                            dve.wait_ge(fx_full, k + 1)
                            if k >= 2:
                                dve.wait_ge(fx_free, k - 1)
                            dve.tensor_tensor_reduce(junk[:, k % 2 * 512:k % 2 * 512 + b - a], banks[k % 2][:, 0:b - a],
                                                     mask[:, t % 2, a:b], 1.0, LEAST, ALU.add, ALU.max,
                                                     mxp[:, h, c:c + 1]).then_inc(fx_free, 1)
                    dve.wait_ge(fx_free, last_fx(t) + 1)
                    link(dve.tensor_reduce(nmax[:], mxp[:, :, 0:nc_], AX.X, ALU.max, negate=True))
                    dve.wait_ge(dk, n)
                    if t >= 2:
                        dve.wait_ge(fl_full, last_fl(t - 2) + 1)
                    for h in range(NH):
                        ins = dve.tensor_scalar(shift[:, t % 2, h, :], identb[:], nmax[:, h:h + 1], None, ALU.mult)
                    ins.then_inc(shift_done, 1)

                def invert_sums(t):
                    dve.wait_ge(sums_out, 4 * (t + 1))
                    dve.reciprocal(den[:, t % 2], den[:, t % 2]).then_inc(recip_done, 1)

                def post_norm(tiles):
                    nonlocal n
                    if not tiles:
                        return
                    a, b = tiles[0], tiles[-1] + 1
                    m = b - a
                    dve.wait_ge(o_free, 4 * b)
                    link(dve.tensor_tensor(root[:, 3, 0:m], ss2[:, a:b, 0], ss2[:, a:b, 1], ALU.add))
                    dve.wait_ge(dk, n)
                    n = inverse_root(dve, dk, n, root[:, 0, 0:m], root[:, 1, 0:m], root[:, 2, 0:m], root[:, 3, 0:m],
                                     1.0 / D)
                    dve.wait_ge(wout_in, 32)
                    for t in tiles:
                        dve.scalar_tensor_tensor(osb[:, t % 2], osb[:, t % 2], root[:, 1, t - a:t - a + 1], gpost[:],
                                                 ALU.mult, ALU.mult).then_inc(post_done, 1)

                for p in range(NGR + 2):
                    before = group(p - 1)
                    if searched(p):
                        search(p, 0)
                    if before:
                        invert_sums(before[0])
                    if searched(p):
                        search(p, 1)
                    post_norm(group(p - 2))
                    if searched(p):
                        search(p, 2)
                        ends(p)
                        set_mask(group(p)[0])
                    for t in before[1:]:
                        invert_sums(t)
                    if searched(p):
                        for t in group(p)[1:]:
                            set_mask(t)
                    for t in group(p):
                        maxima(t)


INPUTS = ["x_prompt", "x_sample", "cache_k", "cache_v", "cache_kidx", "state_pool", "rel_bias", "g_pre", "w_in",
          "w_pool", "pool_scale", "w_out", "g_post"]
OUTPUTS = {
    "y_prompt": (1, SEQ, D), "y_sample": (1, DEC, D),
    "new_k_prompt": (1, 1, SEQ, NKV, HD), "new_v_prompt": (1, 1, SEQ, NKV, HD),
    "new_kidx_prompt": (1, 1, SEQ, DI), "new_pool_prompt": (1, 1, HIST, DPOOL),
    "new_k_sample": (1, 1, DEC, NKV, HD), "new_v_sample": (1, 1, DEC, NKV, HD),
    "new_kidx_sample": (1, 1, DEC, DI), "new_pool_sample": (1, 1, HIST, DPOOL),
}


def tables():
    rel = P - 1 - np.arange(GLEN)
    half = NBUCKETS // 2
    exact = half // 2
    n = np.abs(rel)
    large = exact + (np.log(np.maximum(n, 1).astype(np.float32) / exact) / np.log(1024 / exact)
                     * (half - exact)).astype(np.int32)
    bucket = np.where(rel > 0, half, 0) + np.where(n < exact, n, np.minimum(large, half - 1))
    assert bucket[-1] == half - 1 and n[-1] >= 558
    onehot = (bucket[None, :] == np.arange(NBUCKETS)[:, None]).astype(np.float32)
    fix = np.ones((P, NG, 16), np.float32)
    for g in range(NG):
        w = 2 << g
        fix[:, g, :] = w / np.minimum(w, np.arange(16) + 1)
    return {"bucket_onehot": onehot, "pool_fix": fix}


def layout(inputs):
    arrays = {n: np.ascontiguousarray(inputs[n]) for n in INPUTS} | tables()
    for n in ("g_pre", "pool_scale"):
        arrays[n] = np.ascontiguousarray(arrays[n].reshape(-1, P).T)
    w = arrays["w_in"]

    def ordered(columns):
        return columns.reshape(1, D, NKV, GRP, HD).transpose(0, 1, 3, 2, 4).reshape(1, D, NH * HD)

    arrays["w_in"] = np.concatenate([w[:, :, :C_Q], ordered(w[:, :, C_Q:C_K]), w[:, :, C_K:C_GB],
                                     ordered(w[:, :, C_GB:])], axis=2)
    w = arrays["w_out"]
    arrays["w_out"] = np.concatenate(
        [w[:, :DPOOL], ordered(w[:, DPOOL:].transpose(0, 2, 1)).transpose(0, 2, 1)], axis=1)
    return arrays


def program(nc, arrays):
    A = {n: nc.dram_tensor(n, a.shape, mybir.dt.from_np(a.dtype), kind="ExternalInput").ap() for n, a in arrays.items()}
    for n, shape in OUTPUTS.items():
        A[n] = nc.dram_tensor(n, shape, F32, kind="ExternalOutput").ap()
    build(nc, A)


def kernel(**inputs):
    import concourse.bacc as bacc
    from concourse.bass_utils import run_bass_kernel_spmd

    nc = bacc.Bacc("TRN2", target_bir_lowering=False, num_devices=1)
    arrays = layout(inputs)
    program(nc, arrays)
    r = run_bass_kernel_spmd(nc, [arrays], core_ids=[0])
    return tuple(r.results[0][n] for n in OUTPUTS)
```

```python
from contextlib import ExitStack

import numpy as np
import concourse.bass as bass
from concourse import mybir

ALU = mybir.AluOpType
ACT = mybir.ActivationFunctionType
AX = mybir.AxisListType
F32 = mybir.dt.float32
F32R = mybir.dt.float32r
BF16 = mybir.dt.bfloat16
F16 = mybir.dt.float16
I32 = mybir.dt.int32
U32 = mybir.dt.uint32

P = 128
D = 1024
DC = D // P
SEQ, DEC, PAST = 2048, 32, 1024
CHUNK = 64
NPT = SEQ // P
ST = NPT
NT = NPT + 1
TOKENS = NT * P
DPOOL, NG = 512, 4
HIST = 15
UOFF = 16
NH, HD, NKV, GRP = 8, 64, 2, 4
NIH, DI = 8, 32
TOPK = 256
NBUCKETS = 32
EPS = 1e-6
ATTN_SCALE = HD ** -0.5
INDEX_SCALE = (DI ** -0.5) * (NIH ** -0.5)
C_U, C_GA, C_Q, C_K, C_V, C_QI, C_KI, C_WI, C_GB = 0, 512, 1024, 1536, 1664, 1792, 2048, 2080, 2088
COLS = 2600
BIAS_TILES = 6
BIAS_W = BIAS_TILES * P
GLEN = BIAS_W + P - 1
MASKED = -1e30
LEAST = -3e38
UNSEEN = -2.0
ROUNDS = (11, 11, 6)
ACT_ROUNDS = 3
ZOOM = 1024
SPAN = 15360.0
REACH = 16384.0
MAGIC = float(0x5F3759DF)

EARLY = range(TOPK // P, 6)
SEARCH_PIECES = [(0, True, 3), (0, False, 4), (0, False, 4), (1, True, 3), (1, False, 4), (1, False, 4),
                 (2, True, 2), (2, False, 4)]
BLOCKS = [(4 * b, 4) for b in range(NPT // 4)] + [(ST, 1)]


def key_tiles(t):
    return t + 1 if t < NPT else PAST // P + 1


def place_of(t):
    return t if t < NPT else PAST // P


def score_chunks(t):
    n = key_tiles(t) * P
    return [(a, min(a + 1024, n)) for a in range(0, n, 1024)]


def phase1_steps():
    steps = [("N", 0), ("N", 1), ("N", 2)]
    inside = {}
    pending = []
    seeking = []

    def spread(k):
        for _ in range(min(k, len(pending))):
            steps.append(pending.pop(0))

    def project(step, k):
        inside[step] = [pending.pop(0) for _ in range(min(k, len(pending), 2 * DC if step[0] == "TM" else DC))]
        steps.extend(inside[step])
        steps.append(step)

    def seek():
        if seeking:
            steps.append(seeking.pop(0))
            if steps[-1][0] == "SM" and seeking:
                steps.append(seeking.pop(0))

    windows = []

    def pool_part():
        while windows:
            b, g = windows.pop(0)
            steps.append(("PD", b, g))
            steps.append(("PL", b, g))

    for b, (t0, nt) in enumerate(BLOCKS):
        for i in range(nt):
            steps.append(("H", t0 + i))
            spread(1)
            seek()
            if i == 0 and nt == 4:
                steps.append(("N", t0 + 3))
        ahead = [BLOCKS[b + 1][0] + i for i in range(min(3, BLOCKS[b + 1][1]))] if b + 1 < len(BLOCKS) else []
        if nt == 1:
            spread(100)
            pool_part()
            steps.append(("HIST",))
            for j in range(PAST // P):
                steps.append(("KC", j))
        for i in range(nt):
            t = t0 + i
            gs = [i] if nt == 4 else range(NG)
            k = -(-len(pending) // 2)
            project(("TM", t), k)
            for g in gs:
                seek()
                project(("GB", b, g), 0)
            pool_part()
            if ahead:
                steps.append(("N", ahead.pop(0)))
            for g in gs:
                project(("Q", b, g), k)
                if nt == 1:
                    pool_part()
                seek()
                project(("GA", b, g), 0)
                seek()
                project(("U", b, g), 0)
                windows.append((b, g))
            spread(100)
            if t - 1 in EARLY:
                seeking.append(("SL", t - 1))
                seeking += [("SP", t - 1, *piece) for piece in SEARCH_PIECES]
                seeking.append(("SM", t - 1))
                if len(seeking) == len(SEARCH_PIECES) + 2:
                    steps.append(seeking.pop(0))
            steps.append(("TR", t))
            pending += [("I", t, h, c) for h in range(NIH) for c in range(len(score_chunks(t)))]
        if b >= len(BLOCKS) - 2:
            steps.append(("NP", b))
    pool_part()
    spread(100)
    while seeking:
        seek()
    return steps, inside


def number(steps):
    fa, fg, fd, fi = {}, {}, {}, {}
    for s in steps:
        k = s[0]
        if k == "H":
            fa["H", s[1], 0] = len(fa)
            fa["H", s[1], 1] = len(fa)
        elif k == "TM":
            fa["TM", s[1], 0] = len(fa)
            fa["TM", s[1], 1] = len(fa)
        elif k in ("Q", "U"):
            fa[s] = len(fa)
        elif k in ("GB", "GA"):
            fg[s] = len(fg)
        elif k == "TR":
            for i in range(3):
                fd["TR", s[1], i] = len(fd)
        elif k in ("PL", "KC", "HIST", "NP"):
            fd[s] = len(fd)
        elif k == "I":
            fi[s] = len(fi)
    return fa, fg, fd, fi


def build(nc, A):
    ctx = ExitStack()
    with ctx:
        keep = {}

        def sb(stack, name, shape, dt):
            return stack.enter_context(nc.sbuf_tensor(name, shape, dt))

        def sem(name):
            return ctx.enter_context(nc.semaphore(name))

        def dram(name, shape, dt=F32):
            return nc.dram_tensor(name, shape, dt, kind="Internal").ap()

        q_dram = dram("q_scratch", (P, GRP, TOKENS))
        gb_dram = dram("gb_scratch", (P, GRP, TOKENS))

        ma_dram = dram("ma_scratch", (P, NG, TOKENS))
        s_dram = dram("s_scratch", (NT, P, SEQ))
        m_dram = dram("mask_scratch", (EARLY[-1] + 1, P, SEQ), BF16)
        g_dram = dram("bias_scratch", (NH, P, GLEN))
        k_dram = dram("sample_keys_scratch", (NKV, P, PAST + P))

        identf = sb(ctx, "identf", [P, P], F32)
        identb = sb(ctx, "identb", [P, P], BF16)
        onesb = sb(ctx, "onesb", [P, P], BF16)
        kT = sb(ctx, "kT", [P, SEQ], F32)
        top = sb(ctx, "top", [P, NT], F32)

        banks = [ctx.enter_context(nc.psum_tensor(f"bank{i}", [P, 512], F32)) for i in range(4)]
        wide = [ctx.enter_context(nc.psum_tensor(f"wide{i}", [P, 1024], F32)) for i in range(2)]

        phase1(nc, A, sb, sem, identf, identb, onesb, kT, top, banks, wide, q_dram, gb_dram, ma_dram, s_dram, m_dram)
        phase2(nc, A, sb, sem, identf, identb, onesb, kT, top, banks, wide, q_dram, gb_dram, ma_dram, s_dram, m_dram,
               g_dram, k_dram)


def inverse_root(dve, done, n, ms, y, tmp, ss, scale):
    dve.tensor_scalar(ms, ss, scale, EPS, ALU.mult, ALU.add).then_inc(done, 1)
    n += 1
    dve.wait_ge(done, n)
    dve.tensor_scalar(y.bitcast(I32), ms.bitcast(I32), -0.5, MAGIC, ALU.mult, ALU.add).then_inc(done, 1)
    n += 1
    for _ in range(3):
        dve.wait_ge(done, n)
        dve.tensor_tensor(tmp, y, ms, ALU.mult).then_inc(done, 1)
        n += 1
        dve.wait_ge(done, n)
        dve.scalar_tensor_tensor(tmp, tmp, -0.5, y, ALU.mult, ALU.mult).then_inc(done, 1)
        n += 1
        dve.wait_ge(done, n)
        dve.scalar_tensor_tensor(y, tmp, 1.5, y, ALU.add, ALU.mult).then_inc(done, 1)
        n += 1
    dve.wait_ge(done, n)
    return n


class Search:

    def __init__(self, sb, st, tiles, keys):
        self.near = sb(st, f"near_s{tiles}", [P, tiles, keys], F16)
        self.above = sb(st, f"above{tiles}", [P, keys], BF16)
        self.reach = sb(st, f"reach{tiles}", [P, keys], BF16)
        self.unit, self.scale, self.centre, self.cand, self.cnt, self.side, self.room, self.lo, self.hi = (
            sb(st, f"search{tiles}_{i}", [P, tiles], F32) for i in range(9))
        self.width = sb(st, f"width{tiles}", [P, 1], F32)


def first_units(dve, done, n, B, top):
    cols = slice(0, top.shape[1])
    dve.memset(B.centre[:, cols], 0.0).then_inc(done, 1)
    dve.tensor_scalar(B.unit[:, cols], top, 1.0 / SPAN, None, ALU.mult).then_inc(done, 1)
    dve.wait_ge(done, n + 2)
    dve.reciprocal(B.scale[:, cols], B.unit[:, cols]).then_inc(done, 1)
    return n + 3


def open_level(dve, done, n, B, level, top, scores):
    m = len(scores)
    cols = slice(0, m)

    def link(ins):
        nonlocal n
        ins.then_inc(done, 1)
        n += 1

    if n:
        dve.wait_ge(done, n)
    if level == 0:
        n = first_units(dve, done, n, B, top)
    else:
        link(dve.tensor_tensor(B.side[:, cols], B.cand[:, cols], B.unit[:, cols], ALU.mult))
        link(dve.tensor_scalar(B.scale[:, cols], B.scale[:, cols], float(ZOOM), None, ALU.mult))
        dve.wait_ge(done, n)
        link(dve.tensor_tensor(B.centre[:, cols], B.centre[:, cols], B.side[:, cols], ALU.add))
        link(dve.tensor_scalar(B.unit[:, cols], B.unit[:, cols], 1.0 / ZOOM, None, ALU.mult))
    link(dve.memset(B.cand[:, cols], 0.0))
    link(dve.memset(B.width[:], 2.0 * REACH))
    dve.wait_ge(done, n)
    if level > 0:
        for edge, sign in ((B.lo, -1), (B.hi, 1)):
            link(dve.scalar_tensor_tensor(edge[:, cols], B.unit[:, cols], sign * 1.5 * REACH, B.centre[:, cols],
                                          ALU.mult, ALU.add))
        dve.wait_ge(done, n)
        for i, s in enumerate(scores):
            link(dve.tensor_scalar(s, s, B.lo[:, i:i + 1], B.hi[:, i:i + 1], ALU.max, ALU.min))
        dve.wait_ge(done, n)
    for i, s in enumerate(scores):
        link(dve.tensor_scalar(B.near[:, i, 0:s.shape[1]], s, B.centre[:, i:i + 1], B.scale[:, i:i + 1],
                               ALU.subtract, ALU.mult))
    return n


def halve(dve, done, n, B, widths, rounds):
    m = len(widths)
    cols = slice(0, m)
    each = m + 3
    with dve.Fori(0, rounds) as r:
        at = r * each + n
        dve.wait_ge(done, at)
        for i, w in enumerate(widths):
            dve.tensor_scalar((B.above, B.reach)[i][:, 0:w], B.near[:, i, 0:w], B.cand[:, i:i + 1], None,
                              ALU.is_ge, ALU.add, accum_out=B.cnt[:, i:i + 1]).then_inc(done, 1)
        dve.tensor_scalar(B.width[:], B.width[:], 0.5, None, ALU.mult).then_inc(done, 1)
        dve.wait_ge(done, at + m)
        dve.tensor_scalar(B.side[:, cols], B.cnt[:, cols], TOPK - 0.5, 0.5, ALU.is_ge, ALU.subtract).then_inc(done, 1)
        dve.wait_ge(done, at + m + 2)
        dve.scalar_tensor_tensor(B.cand[:, cols], B.side[:, cols], B.width[:], B.cand[:, cols], ALU.mult, ALU.add)\
           .then_inc(done, 1)
    return n + each * rounds


def choose(dve, done, n, B, i, w):

    def link(ins):
        nonlocal n
        ins.then_inc(done, 1)
        n += 1

    half = REACH / 2.0 ** ROUNDS[-1]
    col = slice(i, i + 1)
    s = B.near[:, i, 0:w]
    dve.wait_ge(done, n)
    link(dve.tensor_scalar(B.lo[:, col], B.cand[:, col], half, None, ALU.subtract))
    link(dve.tensor_scalar(B.hi[:, col], B.cand[:, col], half, None, ALU.add))
    dve.wait_ge(done, n)
    link(dve.tensor_scalar(B.above[:, 0:w], s, B.hi[:, col], None, ALU.is_ge, ALU.add, accum_out=B.cnt[:, col]))
    link(dve.tensor_scalar(B.reach[:, 0:w], s, B.lo[:, col], None, ALU.is_ge))
    dve.wait_ge(done, n)
    link(dve.tensor_scalar(B.room[:, col], B.cnt[:, col], -1.0, float(TOPK), ALU.mult, ALU.add))
    link(dve.tensor_tensor_scan(s, B.reach[:, 0:w], B.above[:, 0:w], 0.0, ALU.add, ALU.subtract))
    link(dve.tensor_tensor(B.above[:, 0:w], B.reach[:, 0:w], B.above[:, 0:w], ALU.add))
    dve.wait_ge(done, n)
    link(dve.scalar_tensor_tensor(B.reach[:, 0:w], s, B.room[:, col], B.above[:, 0:w],
                                  ALU.is_gt, ALU.is_ge))
    dve.wait_ge(done, n)
    return n


def phase1(nc, A, sb, sem, identf, identb, onesb, kT, top, banks, wide, q_dram, gb_dram, ma_dram, s_dram, m_dram):
    steps, inside = phase1_steps()
    in_projection = {piece for pieces in inside.values() for piece in pieces}
    fa, fg, fd, fi = number(steps)
    norm_order = {s[1]: i for i, s in enumerate(x for x in steps if x[0] == "N")}
    pool_order = {s[1:]: i for i, s in enumerate(x for x in steps if x[0] == "PL")}
    with ExitStack() as st:
        W = sb(st, "W", [P, DC, COLS], F32)
        gpre = sb(st, "gpre", [P, DC], F32)
        pscale = sb(st, "pscale", [P, NG], F32)
        wpool = sb(st, "wpool", [P, NG, P], F32)
        fix = sb(st, "fix", [P, NG, 16], F32)
        xs = sb(st, "xs", [P, 3, D], F32)
        junk = sb(st, "junk", [P, D], BF16)
        ss = sb(st, "ss", [P, NT], F32)
        small = sb(st, "small", [P, 4], F32)
        hT = sb(st, "hT", [P, DC, 512], F32)
        kq = sb(st, "kq", [P, 2, 552], F32)
        qs = sb(st, "qs", [P, NIH, 3 * DI], F32)
        ks = sb(st, "ks", [P, 3 * DI], F32)
        wi = sb(st, "wi", [P, 2, NIH], F32)
        qiT = sb(st, "qiT", [3 * DI, 2, NIH, P], F32R)
        kiT = sb(st, "kiT", [3 * DI, SEQ], F32R)
        relu = sb(st, "relu", [P, 2, 1024], F32)
        S = sb(st, "S", [P, 2, SEQ], F32)
        gst = sb(st, "gst", [P, 2, 512], F32)
        sga = sb(st, "sga", [P, 2, 512], F32)
        qst = sb(st, "qst", [P, 2, 512], F32)
        U = sb(st, "U", [P, NG, UOFF + 512], F32)
        win = sb(st, "win", [P, 2, UOFF + 512], F32)
        B = Search(sb, st, 1, key_tiles(EARLY[-1]) * P)
        Se = sb(st, "Se", [P, key_tiles(EARLY[-1]) * P], F32)
        rows = sb(st, "rows", [HIST, DPOOL], F32)

        x_in = [sem(f"x_in{i}") for i in range(3)]
        wa_in = [sem(f"wa_in{c}") for c in range(DC)]
        wb_in = [sem(f"wb_in{c}") for c in range(DC)]
        gpre_in = sem("gpre_in")
        small_in = sem("small_in")
        kc_in = sem("kc_in")
        w_scaled = sem("w_scaled")
        ident_done = sem("ident_done")
        x_zeroed = sem("x_zeroed")
        ss_done = sem("ss_done")
        dve_chain = sem("dve_chain")
        h_ready = sem("h_ready")
        fa_full, fa_free = sem("fa_full"), sem("fa_free")
        fg_full, fg_tanh, fg_free = sem("fg_full"), sem("fg_tanh"), sem("fg_free")
        fd_full, fd_free = sem("fd_full"), sem("fd_free")
        fi_full, fi_free = sem("fi_full"), sem("fi_free")
        relu_used = sem("relu_used")
        split_done = sem("split_done")
        kc_split = sem("kc_split")
        kq_out = [sem(f"kq_out{i}") for i in range(2)]
        gst_out = [sem(f"gst_out{i}") for i in range(2)]
        qst_out = [sem(f"qst_out{i}") for i in range(2)]
        u_ready = sem("u_ready")
        win_chain = sem("win_chain")
        d_ready = sem("d_ready")
        np_out = sem("np_out")
        hist_in = sem("hist_in")
        s_ready = sem("s_ready")
        kT_done = sem("kT_done")
        Se_in, m_ready, m_out = sem("Se_in"), sem("m_ready"), sem("m_out")
        s_out = [sem(f"s_out{i}") for i in range(2)]

        g_stores = [s for s in steps if s[0] in ("GB", "PL")]
        g_slot = {s: i for i, s in enumerate(g_stores)}
        q_slot = {s: i for i, s in enumerate(x for x in steps if x[0] == "Q")}
        tm_order = {s[1]: i for i, s in enumerate(x for x in steps if x[0] == "TM")}
        n_kc = PAST // P
        kc = xs[:, norm_order[ST - 2] % 3, 0:n_kc * DI].rearrange("p (j d) -> p j d", d=DI)

        def width(b):
            return BLOCKS[b][1] * P

        win_end, total = {}, 0
        for s in steps:
            if s[0] == "PL":
                total += s[2] + 1 + (s[1] == 0)
                win_end[s[1:]] = total

        with nc.Block() as block:
            @block.sync
            def _(sp):
                def load_x(i, t):
                    if i >= 3:
                        prev = [u for u in norm_order if norm_order[u] == i - 3][0]
                        sp.wait_ge(fa_full, fa["H", prev, 1] + 1)
                    if t == ST:
                        sp.wait_ge(x_zeroed, 1)
                        sp.dma_start(xs[0:DEC, i % 3, :], A["x_sample"][0]).then_inc(x_in[i % 3], 16)
                    else:
                        sp.dma_start(xs[:, i % 3, :], A["x_prompt"][0, t * P:(t + 1) * P, :]).then_inc(x_in[i % 3], 16)

                order = sorted(norm_order, key=norm_order.get)
                for i in range(3):
                    load_x(i, order[i])
                sp.dma_start(gpre[:], A["g_pre"]).then_inc(gpre_in, 16)
                w_rows = A["w_in"][0].rearrange("(c p) n -> c p n", p=P)
                for c in range(DC):
                    sp.dma_start(W[:, c, C_K:COLS], w_rows[c, :, C_K:COLS]).then_inc(wa_in[c], 16)
                for c in range(DC):
                    sp.dma_start(W[:, c, 0:C_K], w_rows[c, :, 0:C_K]).then_inc(wb_in[c], 16)
                sp.dma_start(pscale[:], A["pool_scale"]).then_inc(small_in, 16)
                sp.dma_start(wpool[:], A["w_pool"][0].rearrange("g c d -> c g d")).then_inc(small_in, 16)
                sp.dma_start(fix[:], A["pool_fix"]).then_inc(small_in, 16)
                loaded = 3
                n_tm = {0: 0, 1: 0}
                for s in steps:
                    if s[0] == "H":
                        if loaded < NT:
                            load_x(loaded, order[loaded])
                            loaded += 1
                    elif s[0] == "HIST":
                        sp.wait_ge(fa_full, fa["H", ST - 2, 1] + 1)
                        sp.dma_start(kc, A["cache_kidx"][0, 0].rearrange("(j p) d -> p j d", p=P)).then_inc(kc_in, 16)
                    elif s[0] == "TM":
                        t = s[1]
                        i = tm_order[t] % 2
                        sp.wait_ge(fa_free, fa["TM", t, 1] + 1)
                        new = "prompt" if t < NPT else "sample"
                        a, b, r = (t * P, t * P + P, P) if t < NPT else (0, DEC, DEC)
                        kk = A[f"new_k_{new}"][0, 0, a:b].rearrange("t k d -> t (k d)")
                        vv = A[f"new_v_{new}"][0, 0, a:b].rearrange("t k d -> t (k d)")
                        sp.dma_start(kk, kq[0:r, i, 0:128]).then_inc(kq_out[i], 16)
                        sp.dma_start(vv, kq[0:r, i, 128:256]).then_inc(kq_out[i], 16)
                        sp.dma_start(A[f"new_kidx_{new}"][0, 0, a:b], kq[0:r, i, 512:544]).then_inc(kq_out[i], 16)
                    elif s[0] in ("GB", "PL"):
                        n = g_slot[s]
                        if s[0] == "GB":
                            sp.wait_ge(fg_free, fg[s] + 1)
                            b, g = s[1:]
                            a = BLOCKS[b][0] * P
                            dst = gb_dram[:, g, a:a + width(b)]
                            src = gst[:, n % 2, 0:width(b)]
                        else:
                            sp.wait_ge(fd_free, fd[s] + 1)
                            b, g = s[1:]
                            a = BLOCKS[b][0] * P
                            dst = ma_dram[:, g, a:a + width(b)]
                            src = gst[:, n % 2, 0:width(b)]
                        sp.dma_start(dst, src).then_inc(gst_out[n % 2], 16)
                    elif s[0] == "Q":
                        n = q_slot[s]
                        b, j = s[1:]
                        a = BLOCKS[b][0] * P
                        sp.wait_ge(fa_free, fa[s] + 1)
                        sp.dma_start(q_dram[:, j, a:a + width(b)], qst[:, n % 2, 0:width(b)])\
                          .then_inc(qst_out[n % 2], 16)
                    elif s[0] == "NP":
                        b = s[1]
                        k = b - (len(BLOCKS) - 2)
                        sp.wait_ge(fd_free, fd[s] + 1)
                        sp.dma_start(A["new_pool_prompt" if k == 0 else "new_pool_sample"][0, 0], rows[:])\
                          .then_inc(np_out, 16)
                        if k == 0:
                            sp.wait_ge(np_out, 16)
                            sp.dma_start(rows[:], A["state_pool"][0, 0]).then_inc(hist_in, 16)
                    elif s[0] == "I" and s[2] == NIH - 1 and s[3] == len(score_chunks(s[1])) - 1:
                        t = s[1]
                        if t < TOPK // P:
                            continue
                        n = key_tiles(t) * P
                        sp.wait_ge(s_ready, t + 1)
                        sp.dma_start(s_dram[t, :, 0:n], S[:, t % 2, 0:n]).then_inc(s_out[t % 2], 16)
                    elif s[0] == "SL":
                        t = s[1]
                        n = key_tiles(t) * P
                        sp.wait_ge(s_out[t % 2], 16 * (t // 2))
                        if t > EARLY[0]:
                            sp.wait_ge(m_ready, t - EARLY[0])
                        sp.dma_start(Se[:, 0:n], s_dram[t, :, 0:n]).then_inc(Se_in, 16)
                    elif s[0] == "SM":
                        t = s[1]
                        n = key_tiles(t) * P
                        sp.wait_ge(m_ready, t - EARLY[0] + 1)
                        sp.dma_start(m_dram[t, :, 0:n], B.reach[:, 0:n]).then_inc(m_out, 16)
                sp.wait_ge(m_out, 16 * len(EARLY))
                for i in range(2):
                    sp.wait_ge(kq_out[i], 48 * len(range(i, NT, 2)))
                    sp.wait_ge(gst_out[i], 16 * len(range(i, len(g_stores), 2)))
                    sp.wait_ge(qst_out[i], 16 * len(range(i, len(q_slot), 2)))
                    sp.wait_ge(s_out[i], 16 * len(range(2 + i, NT, 2)))
                sp.wait_ge(np_out, 32)

            @block.gpsimd
            def _(pool):
                pool.memset(identf[:], 0.0).then_inc(ident_done, 1)
                pool.memset(identb[:], 0.0).then_inc(ident_done, 1)
                pool.memset(onesb[:], 1.0).then_inc(ident_done, 1)
                pool.memset(U[:, :, 0:UOFF], 0.0).then_inc(ident_done, 1)
                pool.wait_ge(ident_done, 4)
                for m in (identf, identb):
                    pool.affine_select(out=m[:], in_=m[:], compare_op=ALU.not_equal, fill=1.0, base=0,
                                       pattern=[[-1, P]], channel_multiplier=1).then_inc(ident_done, 1)
                chain = 0
                for s in steps:
                    if s == ("H", ST - 3):
                        i = norm_order[ST]
                        prev = [u for u in norm_order if norm_order[u] == i - 3][0]
                        pool.wait_ge(fa_full, fa["H", prev, 1] + 1)
                        pool.memset(xs[:, i % 3, :], 0.0).then_inc(x_zeroed, 1)
                    elif s[0] == "PL":
                        b, g = s[1:]
                        w = 2 << g
                        T = width(b)
                        k = pool_order[b, g]
                        pool.wait_ge(fa_free, fa["U", b, g] + 1)
                        if b == len(BLOCKS) - 1:
                            pool.wait_ge(fd_free, fd["HIST",] + 1)
                        if k >= 1:
                            prev = [u for u in pool_order if pool_order[u] == k - 1][0]
                            pool.wait_ge(fd_full, fd["PL", *prev] + 1)
                        src = U[:, g, :]
                        step, level = 1, 0
                        while step < w:
                            a = UOFF - (w - 2 * step)
                            dst = win[:, level % 2, :]
                            if level:
                                pool.wait_ge(win_chain, chain)
                            pool.tensor_tensor(dst[:, a:UOFF + T], src[:, a:UOFF + T],
                                               src[:, a - step:UOFF + T - step], ALU.add).then_inc(win_chain, 1)
                            chain += 1
                            src = dst
                            step *= 2
                            level += 1
                        if b == 0:
                            pool.wait_ge(win_chain, chain)
                            pool.tensor_tensor(src[:, UOFF:UOFF + HIST], src[:, UOFF:UOFF + HIST],
                                               fix[:, g, 0:HIST], ALU.mult).then_inc(win_chain, 1)
                            chain += 1
                        if b < len(BLOCKS) - 2:
                            pool.wait_ge(d_ready, k + 1)
                            pool.tensor_copy(U[:, g, 1:UOFF], U[:, g, T + 1:T + UOFF]).then_inc(u_ready, 1)

            @block.scalar
            def _(act):
                for s in steps:
                    if s[0] == "N":
                        t = s[1]
                        i = norm_order[t]
                        act.wait_ge(x_in[i % 3], 16 * (i // 3 + 1))
                        if i:
                            act.wait_ge(ss_done, i)
                        act.activation(junk[:], xs[:, i % 3, :], ACT.Square, accum_out=ss[:, t:t + 1])\
                           .then_inc(ss_done, 1)
                    elif s[0] == "H":
                        t = s[1]
                        for half in range(2):
                            k = fa["H", t, half]
                            act.wait_ge(fa_full, k + 1)
                            tt = (t % 4) * P
                            act.activation(hT[:, 4 * half:4 * half + 4, tt:tt + P],
                                           banks[k % 2][:].rearrange("p (c n) -> p c n", c=4), ACT.Copy)\
                               .then_inc(fa_free, 1)
                    elif s[0] == "TM":
                        t = s[1]
                        o = tm_order[t]
                        for part, (a, b) in enumerate(((0, 256), (256, 552))):
                            k = fa["TM", t, part]
                            act.wait_ge(fa_full, k + 1)
                            if part == 0 and o >= 2:
                                act.wait_ge(kq_out[o % 2], 48 * (o // 2))
                                act.wait_ge(split_done, 5 * (o - 1))
                                act.wait_ge(fd_full, fd["TR", o - 2, 0] + 1)
                            act.activation(kq[:, o % 2, a:b], banks[k % 2][:, 0:b - a], ACT.Copy)\
                               .then_inc(fa_free, 1)
                    elif s[0] == "Q":
                        k, n, T = fa[s], q_slot[s], width(s[1])
                        act.wait_ge(fa_full, k + 1)
                        if n >= 2:
                            act.wait_ge(qst_out[n % 2], 16 * (n // 2))
                        act.activation(qst[:, n % 2, 0:T], banks[k % 2][:, 0:T], ACT.Copy, scale=ATTN_SCALE)\
                           .then_inc(fa_free, 1)
                    elif s[0] == "U":
                        b, g = s[1:]
                        k, T = fa[s], width(b)
                        act.wait_ge(fa_full, k + 1)
                        if 1 <= b < len(BLOCKS) - 1:
                            act.wait_ge(u_ready, pool_order[b - 1, g] + 1)
                        if b == len(BLOCKS) - 1:
                            act.wait_ge(fd_full, fd["NP", b - 1] + 1)
                            act.wait_ge(d_ready, pool_order[b - 1, g] + 1)
                        act.activation(U[:, g, UOFF:UOFF + T], banks[k % 2][:, 0:T], ACT.Copy).then_inc(fa_free, 1)
                    elif s[0] in ("GB", "GA"):
                        k = fg[s]
                        T = width(s[1])
                        act.wait_ge(fg_full, k + 1)
                        if s[0] == "GB":
                            m = g_slot[s]
                            dst = gst[:, m % 2, 0:T]
                            if m >= 2:
                                act.wait_ge(gst_out[m % 2], 16 * (m // 2))
                        else:
                            m = pool_order[s[1:]]
                            dst = sga[:, m % 2, 0:T]
                            if m >= 2:
                                prev = [u for u in pool_order if pool_order[u] == m - 2][0]
                                act.wait_ge(fd_free, fd["PL", *prev] + 1)
                        act.activation(dst, banks[2][:, 0:T], ACT.Tanh, scale=0.5).then_inc(fg_tanh, 1)
                    elif s[0] == "TR":
                        t = s[1]
                        k = fd["TR", t, 0]
                        act.wait_ge(fd_full, k + 1)
                        if t < NPT:
                            act.activation(kT[:, t * P:(t + 1) * P], banks[3][:, 0:P], ACT.Copy).then_inc(kT_done, 1)
                        at = place_of(t) * P
                        if t == ST:
                            act.wait_ge(fd_free, fd["KC", n_kc - 1] + 1)
                        act.activation(kiT[:, at:at + P], banks[3][0:3 * DI, P:2 * P], ACT.Copy).then_inc(fd_free, 1)
                        for half in range(2):
                            act.wait_ge(fd_full, k + 2 + half)
                            act.activation(qiT[:, t % 2, 4 * half:4 * half + 4, :],
                                           banks[3][0:3 * DI, :].rearrange("p (h n) -> p h n", h=4), ACT.Copy)\
                               .then_inc(fd_free, 1)
                    elif s[0] == "I":
                        k = fi[s]
                        a, b = score_chunks(s[1])[s[3]]
                        act.wait_ge(fi_full, k + 1)
                        if k >= 2:
                            act.wait_ge(relu_used, k - 1)
                        act.activation(relu[:, k % 2, 0:b - a], wide[k % 2][:, 0:b - a], ACT.Relu)\
                           .then_inc(fi_free, 1)

            @block.tensor
            def _(pe):
                def fa_bank(key):
                    k = fa[key]
                    if k >= 2:
                        pe.wait_ge(fa_free, k - 1)
                    return banks[k % 2]

                def fd_bank(key):
                    k = fd[key]
                    if k >= 1:
                        pe.wait_ge(fd_free, k)
                    return banks[3]

                def contract(out, stationary, moving, pieces=()):
                    for c in range(DC):
                        mm = pe.matmul(out, stationary(c), moving(c), start=(c == 0), stop=(c == DC - 1))
                        if c < DC - 1:
                            for piece in pieces[c * len(pieces) // (DC - 1):(c + 1) * len(pieces) // (DC - 1)]:
                                score(*piece)
                    return mm

                def score(_, t, h, c):
                    k = fi["I", t, h, c]
                    a, b = score_chunks(t)[c]
                    if k >= 2:
                        pe.wait_ge(fi_free, k - 1)
                    pe.wait_ge(fd_free, fd["TR", t, 2] + 1)
                    for x in range(a, b, 512):
                        y = min(x + 512, b)
                        mm = pe.matmul(wide[k % 2][:, x - a:y - a], qiT[:, t % 2, h, :], kiT[:, x:y],
                                       start=True, stop=True)
                    mm.then_inc(fi_full, 1)

                pe.wait_ge(ident_done, 6)
                for s in steps:
                    if s[0] == "H":
                        t = s[1]
                        i = norm_order[t]
                        pe.wait_ge(h_ready, i + 1)
                        for half in range(2):
                            bank = fa_bank(("H", t, half))
                            for c in range(4):
                                col = (4 * half + c) * P
                                tr = pe.transpose(bank[:, c * P:(c + 1) * P], xs[:, i % 3, col:col + P], identf[:])
                            tr.then_inc(fa_full, 1)
                        last_h = fa["H", t, 1]
                    elif s[0] == "TM":
                        t = s[1]
                        tt = (t % 4) * P
                        pe.wait_ge(w_scaled, DC)
                        for part, (a, b) in enumerate(((C_K, C_QI), (C_QI, C_GB))):
                            bank = fa_bank(("TM", t, part))
                            pe.wait_ge(fa_free, last_h + 1)
                            pieces = inside[s][part * len(inside[s]) // 2:(part + 1) * len(inside[s]) // 2]
                            contract(bank[:, 0:b - a], lambda c: hT[:, c, tt:tt + P], lambda c: W[:, c, a:b], pieces)\
                                .then_inc(fa_full, 1)
                    elif s[0] in ("Q", "GA", "U", "GB"):
                        b, g = s[1:]
                        T = width(b)
                        if s[0] != "GB":
                            pe.wait_ge(w_scaled, 2 * DC)
                        if s[0] in ("GA", "GB"):
                            k = fg[s]
                            if k:
                                pe.wait_ge(fg_free, k)
                            bank, full = banks[2], fg_full
                        else:
                            bank, full = fa_bank(s), fa_full
                        base = {"Q": C_Q, "GA": C_GA, "U": C_U, "GB": C_GB}[s[0]] + g * P
                        contract(bank[:, 0:T], lambda c: W[:, c, base:base + P], lambda c: hT[:, c, 0:T],
                                 inside[s]).then_inc(full, 1)
                    elif s[0] == "TR":
                        t = s[1]
                        o = tm_order[t]
                        bank = fd_bank(("TR", t, 0))
                        pe.wait_ge(split_done, 5 * (o + 1))
                        pe.transpose(bank[:, 0:P], kq[:, o % 2, 0:P], identf[:])
                        pe.transpose(bank[0:3 * DI, P:2 * P], ks[:], identf[:]).then_inc(fd_full, 1)
                        for half in range(2):
                            bank = fd_bank(("TR", t, 1 + half))
                            for h in range(4):
                                tr = pe.transpose(bank[0:3 * DI, h * P:(h + 1) * P], qs[:, 4 * half + h, :],
                                                  identf[:])
                            tr.then_inc(fd_full, 1)
                    elif s[0] == "KC":
                        j = s[1]
                        bank = fd_bank(s)
                        pe.wait_ge(kc_split, 3 * (j + 1))
                        pe.transpose(bank[0:3 * DI, 0:P], ks[:], identf[:]).then_inc(fd_full, 1)
                    elif s[0] == "HIST":
                        bank = fd_bank(s)
                        pe.wait_ge(hist_in, 16)
                        for g in range(NG):
                            tr = pe.transpose(bank[:, g * 16:g * 16 + HIST], rows[:, g * P:(g + 1) * P],
                                              identf[0:HIST, 0:HIST])
                        tr.then_inc(fd_full, 1)
                    elif s[0] == "NP":
                        b = s[1]
                        bank = fd_bank(s)
                        last = UOFF + (512 if b < len(BLOCKS) - 1 else DEC)
                        for g in range(NG):
                            pe.wait_ge(fa_free, fa["U", b, g] + 1)
                            tr = pe.transpose(bank[0:HIST, g * P:(g + 1) * P], U[:, g, last - HIST:last], identf[:])
                        tr.then_inc(fd_full, 1)
                    elif s[0] == "PL":
                        b, g = s[1:]
                        T = width(b)
                        bank = fd_bank(s)
                        pe.wait_ge(small_in, 48)
                        pe.wait_ge(d_ready, pool_order[b, g] + 1)
                        fin = win[:, g % 2, UOFF:UOFF + T]
                        pe.matmul(bank[:, 0:T], wpool[:, g, :], fin, start=True, stop=True).then_inc(fd_full, 1)
                    elif s[0] == "I" and s not in in_projection:
                        score(*s)

            @block.vector
            def _(dve):
                n = 0
                scaled = 0

                def scale_w(sems, a, b):
                    dve.wait_ge(gpre_in, 16)
                    for c in range(DC):
                        dve.wait_ge(sems[c], 16)
                        dve.tensor_scalar(W[:, c, a:b], W[:, c, a:b], gpre[:, c:c + 1], None, ALU.mult)\
                           .then_inc(w_scaled, 1)

                for s in steps:
                    if s[0] == "N":
                        t = s[1]
                        i = norm_order[t]
                        dve.wait_ge(ss_done, i + 1)
                        n = inverse_root(dve, dve_chain, n, small[:, 0:1], small[:, 1:2], small[:, 2:3],
                                         ss[:, t:t + 1], 1.0 / D)
                        dve.tensor_scalar(xs[:, i % 3, :], xs[:, i % 3, :], small[:, 1:2], None, ALU.mult)\
                           .then_inc(h_ready, 1)
                        if scaled == 0 and i == 2:
                            scale_w(wa_in, C_K, COLS)
                            scaled = 1
                    elif s[0] == "TM":
                        if scaled == 1:
                            scale_w(wb_in, 0, C_K)
                            dve.wait_ge(small_in, 48)
                            dve.tensor_scalar(pscale[:], pscale[:], 0.5, None, ALU.mult).then_inc(w_scaled, 1)
                            scaled = 2
                        t = s[1]
                        o = tm_order[t]
                        dve.wait_ge(fa_free, fa["TM", t, 1] + 1)
                        if o >= 1:
                            dve.wait_ge(fd_full, fd["TR", o - 1, 2] + 1)
                        if t == ST:
                            dve.wait_ge(fd_full, fd["KC", n_kc - 1] + 1)
                        qi = kq[:, o % 2, 256:512].rearrange("p (h d) -> p h d", h=NIH)
                        ki = kq[:, o % 2, 512:544]
                        dve.tensor_copy(qs[:, :, 0:DI].bitcast(F32R), qi).then_inc(dve_chain, 1)
                        dve.tensor_copy(qs[:, :, DI:2 * DI].bitcast(F32R), qi).then_inc(split_done, 1)
                        dve.tensor_copy(ks[:, 0:DI].bitcast(F32R), ki).then_inc(dve_chain, 1)
                        dve.tensor_copy(ks[:, 2 * DI:3 * DI].bitcast(F32R), ki).then_inc(split_done, 1)
                        if o >= 2:
                            dve.wait_ge(s_ready, o - 1)
                        dve.tensor_scalar(wi[:, o % 2, :], kq[:, o % 2, 544:552], INDEX_SCALE, None, ALU.mult)\
                           .then_inc(split_done, 1)
                        n += 2
                        dve.wait_ge(dve_chain, n)
                        dve.tensor_tensor(qs[:, :, 2 * DI:3 * DI], qi, qs[:, :, 0:DI], ALU.subtract)\
                           .then_inc(split_done, 1)
                        dve.tensor_tensor(ks[:, DI:2 * DI], ki, ks[:, 0:DI], ALU.subtract).then_inc(split_done, 1)
                    elif s[0] == "KC":
                        j = s[1]
                        dve.wait_ge(kc_in, 16)
                        if j == 0:
                            dve.wait_ge(fd_full, fd["TR", NPT - 1, 2] + 1)
                        else:
                            dve.wait_ge(fd_full, fd["KC", j - 1] + 1)
                        dve.tensor_copy(ks[:, 0:DI].bitcast(F32R), kc[:, j, :]).then_inc(kc_split, 1)
                        dve.tensor_copy(ks[:, 2 * DI:3 * DI].bitcast(F32R), kc[:, j, :]).then_inc(kc_split, 1)
                        dve.wait_ge(kc_split, 3 * j + 2)
                        dve.tensor_tensor(ks[:, DI:2 * DI], kc[:, j, :], ks[:, 0:DI], ALU.subtract)\
                           .then_inc(kc_split, 1)
                        if j == 0:
                            last = ("I", NPT - 1, NIH - 1, len(score_chunks(NPT - 1)) - 1)
                            dve.wait_ge(fi_full, fi[last] + 1)
                        dve.wait_ge(fd_full, fd[s] + 1)
                        dve.tensor_copy(kiT[:, j * P:(j + 1) * P], banks[3][0:3 * DI, 0:P]).then_inc(fd_free, 1)
                    elif s[0] == "HIST":
                        dve.wait_ge(fd_full, fd[s] + 1)
                        dve.wait_ge(d_ready, pool_order[len(BLOCKS) - 2, NG - 1] + 1)
                        dve.tensor_copy(U[:, :, 1:UOFF], banks[3][:, 0:64].rearrange("p (g r) -> p g r", g=NG)
                                        [:, :, 0:HIST]).then_inc(fd_free, 1)
                    elif s[0] == "NP":
                        dve.wait_ge(fd_full, fd[s] + 1)
                        dve.tensor_copy(rows[:], banks[3][0:HIST, :]).then_inc(fd_free, 1)
                    elif s[0] in ("GB", "GA"):
                        k = fg[s]
                        T = width(s[1])
                        dve.wait_ge(fg_tanh, k + 1)
                        if s[0] == "GB":
                            dst = gst[:, g_slot[s] % 2, 0:T]
                        else:
                            dst = sga[:, s[2] % 2, 0:T]
                        dve.scalar_tensor_tensor(dst, dst, 1.0, banks[2][:, 0:T], ALU.add, ALU.mult)\
                           .then_inc(fg_free, 1)
                    elif s[0] == "PD":
                        b, g = s[1:]
                        T = width(b)
                        dve.wait_ge(win_chain, win_end[b, g])
                        fin = win[:, g % 2, UOFF:UOFF + T]
                        dve.scalar_tensor_tensor(fin, fin, 1.0 / (2 << g), U[:, g, UOFF:UOFF + T], ALU.mult,
                                                 ALU.subtract).then_inc(d_ready, 1)
                    elif s[0] == "PL":
                        b, g = s[1:]
                        T = width(b)
                        m = g_slot[s]
                        if m >= 2:
                            dve.wait_ge(gst_out[m % 2], 16 * (m // 2))
                        dve.wait_ge(fd_full, fd[s] + 1)
                        dve.wait_ge(fg_free, fg["GA", b, g] + 1)
                        dve.wait_ge(w_scaled, 2 * DC + 1)
                        dve.scalar_tensor_tensor(gst[:, m % 2, 0:T], banks[3][:, 0:T], pscale[:, g:g + 1],
                                                 sga[:, g % 2, 0:T], ALU.mult, ALU.mult).then_inc(fd_free, 1)
                    elif s[0] == "SP":
                        _, t, level, opens, rounds = s
                        w = key_tiles(t) * P
                        if opens:
                            if level == 0:
                                dve.wait_ge(Se_in, 16 * (t - EARLY[0] + 1))
                            n = open_level(dve, dve_chain, n, B, level, top[:, t:t + 1], [Se[:, 0:w]])
                        n = halve(dve, dve_chain, n, B, [w], rounds)
                    elif s[0] == "SM":
                        t = s[1]
                        w = key_tiles(t) * P
                        if t > EARLY[0]:
                            dve.wait_ge(m_out, 16 * (t - EARLY[0]))
                        n = choose(dve, dve_chain, n, B, 0, w)
                        dve.tensor_scalar(B.reach[:, 0:w], B.reach[:, 0:w], MASKED, None, ALU.mult)\
                           .then_inc(m_ready, 1)
                    elif s[0] == "I":
                        _, t, h, c = s
                        k = fi[s]
                        a, b = score_chunks(t)[c]
                        dve.wait_ge(fi_free, k + 1)
                        if h == 0 and t >= 4:
                            dve.wait_ge(s_out[t % 2], 16 * (t // 2 - 1))
                        w = wi[:, t % 2, h:h + 1]
                        if h == 0:
                            dve.tensor_scalar(S[:, t % 2, a:b], relu[:, k % 2, 0:b - a], w, None, ALU.mult)\
                               .then_inc(relu_used, 1)
                        else:
                            dve.wait_ge(relu_used, fi["I", t, h - 1, c] + 1)
                            dve.scalar_tensor_tensor(S[:, t % 2, a:b], relu[:, k % 2, 0:b - a], w,
                                                     S[:, t % 2, a:b], ALU.mult, ALU.add).then_inc(relu_used, 1)
                        if h == NIH - 1 and c == len(score_chunks(t)) - 1:
                            nk = key_tiles(t) * P
                            dve.wait_ge(relu_used, k + 1)
                            dve.tensor_reduce(small[:, 0:1], S[:, t % 2, 0:nk], AX.X, ALU.min)\
                               .then_inc(dve_chain, 1)
                            dve.tensor_reduce(small[:, 1:2], S[:, t % 2, 0:nk], AX.X, ALU.max)\
                               .then_inc(dve_chain, 1)
                            n += 2
                            dve.wait_ge(dve_chain, n)
                            dve.scalar_tensor_tensor(small[:, 2:3], small[:, 0:1], -1.0, small[:, 1:2], ALU.mult,
                                                     ALU.max).then_inc(dve_chain, 1)
                            n += 1
                            dve.wait_ge(dve_chain, n)
                            dve.tensor_scalar(top[:, t:t + 1], small[:, 2:3], 1e-20, None, ALU.max)\
                               .then_inc(dve_chain, 1)
                            dve.tensor_scalar(small[:, 3:4], small[:, 2:3], 1e-20, UNSEEN, ALU.max, ALU.mult)\
                               .then_inc(dve_chain, 1)
                            n += 2
                            dve.wait_ge(dve_chain, n)
                            blind, a = (slice(0, CHUNK), nk - CHUNK) if t < NPT else (slice(0, P), PAST + DEC)
                            dve.tensor_scalar(S[blind, t % 2, a:nk], S[blind, t % 2, a:nk], 0.0, small[blind, 3:4],
                                              ALU.mult, ALU.add).then_inc(s_ready, 1)


def phase2(nc, A, sb, sem, identf, identb, onesb, kT, top, banks, wide, q_dram, gb_dram, ma_dram, s_dram, m_dram,
           g_dram, k_dram):
    groups = [(t, t + 1) for t in range(0, NPT, 2)] + [(ST,)]
    NGR = len(groups)

    def group(p):
        return groups[p] if 0 <= p < NGR else ()

    def chunks(t):
        n = key_tiles(t) * P
        return [(a, min(a + 512, n)) for a in range(0, n, 512)]

    def near(t, kt):
        return place_of(t) - kt < BIAS_TILES

    fx, fl, near_count = {}, {}, {}
    n_near = 0
    for t in range(NT):
        for h in range(NH):
            for c in range(len(chunks(t))):
                fx[t, h, c] = len(fx)
        for kv in range(NKV):
            for kt in range(key_tiles(t)):
                fl[t, kv, kt] = len(fl)
                n_near += near(t, kt)
                near_count[t, kv, kt] = n_near

    def jobs(p):
        return [(t, kv, kt) for t in group(p) for kv in range(NKV) for kt in range(key_tiles(t))]

    def last_fl(t, kv=NKV - 1):
        return fl[t, kv, key_tiles(t) - 1]

    def last_fx(t):
        return fx[t, NH - 1, len(chunks(t)) - 1]

    sample_keys = ((banks[2], 0, 4), (banks[3], 4, 8), (wide[1], 8, 9))
    NSK = PAST // P + 1

    def searched(p):
        return len(group(p)) > 0 and group(p)[0] > EARLY[-1]

    FIRST = next(p for p in range(NGR) if searched(p))

    with ExitStack() as st:
        k2 = [sb(st, f"k2_{kv}", [P, SEQ], F32R) for kv in range(NKV)]
        vx = sb(st, "vx", [P, NPT, 3, HD], F32)
        EB = sb(st, "EB", [P, NH, BIAS_W], F32)
        relb = sb(st, "relb", [NBUCKETS, NH], F32)
        nfar = sb(st, "nfar", [NH, 1], F32)
        wout = sb(st, "wout", [P, DC, D], F32)
        gpost = sb(st, "gpost", [P, D], F32)
        S = sb(st, "S2", [P, 2, SEQ], F32)
        B = Search(sb, st, 2, SEQ)
        mask = sb(st, "mask", [P, 2, SEQ], BF16)
        act_junk = sb(st, "act_junk", [P, SEQ], BF16)
        act_sum, act_side, minus_cand = (sb(st, f"act_search{i}", [P, 2], F32) for i in range(3))
        enough = sb(st, "enough", [P, NT], F32)
        junk = B.above
        q = sb(st, "q", [P, NKV, GRP, P], F32)
        qh = sb(st, "qh", [P, 2, NKV, GRP, P], F32R)
        ql = sb(st, "ql", [P, 2, NKV, GRP, P], F32R)
        gb = sb(st, "gb", [P, 2, 512], F32)
        ma = sb(st, "ma", [P, 2, NG, P], F32)
        xr = sb(st, "xr", [P, 2, D], F32)
        E = sb(st, "E", [P, 4, GRP, P], F32)
        shift = sb(st, "shift", [P, 2, NH, P], BF16)
        osum = sb(st, "osum", [P, 2, 512], F32)
        den = sb(st, "den", [P, 2, 512], F32)
        yT = sb(st, "yT", [P, 2, 4, P], F32)
        sq = sb(st, "sq", [P, 512], BF16)
        mxp = sb(st, "mxp", [P, NH, 4], F32)
        nmax = sb(st, "nmax", [P, NH], F32)
        ss2 = sb(st, "ss2", [P, NT, 2], F32)
        root = sb(st, "root", [P, 4, 2], F32)
        klow = kT[:].bitcast(F32R)
        osb = kT[:].rearrange("p (a n) -> p a n", a=2)
        flat = wout[:].rearrange("p c n -> p (c n)")
        ks_high = flat[:, 0:NSK * P].bitcast(F32R)
        ks_low = flat[:, NSK * P:2 * NSK * P].bitcast(F32R)
        ck = S[:, 1, 0:NSK * P].rearrange("p (j n) -> p j n", n=NKV * HD)
        scratch = B.near[:].rearrange("p a n -> p (a n)").bitcast(F32)
        onehot = scratch[0:NBUCKETS, 0:GLEN]
        G = scratch[0:NH, GLEN:2 * GLEN]

        bias_in, bias_out = sem("bias_in"), sem("bias_out")
        eb_in = sem("eb_in")
        ck_in, ck_zeroed = sem("ck_in"), sem("ck_zeroed")
        wout_in = sem("wout_in")
        S_in = [sem(f"S_in{i}") for i in range(2)]
        S_used = sem("S_used")
        mask_in = [sem(f"mask_in{i}") for i in range(2)]
        q_in, q_split = sem("q_in"), sem("q_split")
        v_in = sem("v_in")
        k_split, k_low, k_moved = sem("k_split"), sem("k_low"), sem("k_moved")
        ks_split, ks_lowered, ks_out, ks_in = sem("ks_split"), sem("ks_lowered"), sem("ks_out"), sem("ks_in")
        gb_in = [sem(f"gb_in{i}") for i in range(2)]
        ma_in = [sem(f"ma_in{i}") for i in range(2)]
        xr_in = [sem(f"xr_in{i}") for i in range(2)]
        y_out = [sem(f"y_out{i}") for i in range(2)]
        g_full, nfar_done, g_exp = sem("g_full"), sem("nfar_done"), sem("g_exp")
        ckt_full = sem("ckt_full")
        dk = sem("dk")
        enough_set = sem("enough_set")
        first_ready, near_made, halved = sem("first_ready"), sem("near_made"), sem("halved")
        mask_done = sem("mask_done")
        plain_mask = sem("plain_mask")
        fx_full, fx_free = sem("fx_full"), sem("fx_free")
        shift_done = sem("shift_done")
        fl_full, fl_free = sem("fl_full"), sem("fl_free")
        biased = sem("biased")
        pv_step = sem("pv_step")
        sums_out, recip_done = sem("sums_out"), sem("recip_done")
        mean_done, yT_done = sem("mean_done"), sem("yT_done")
        o_full, o_free = sem("o_full"), sem("o_free")
        post_done = sem("post_done")
        res_done = sem("res_done")

        with nc.Block() as block:
            @block.sync
            def _(sp):
                def load_S(p):
                    if not searched(p):
                        return
                    if p > FIRST:
                        sp.wait_ge(S_used, p - FIRST)
                    for i, t in enumerate(group(p)):
                        n = key_tiles(t) * P
                        sp.dma_start(S[:, i, 0:n], s_dram[t, :, 0:n]).then_inc(S_in[i], 16)

                def load_mask(t):
                    if t in EARLY:
                        sp.wait_ge(fl_full, last_fl(t - 2) + 1)
                        n = key_tiles(t) * P
                        sp.dma_start(mask[:, t % 2, 0:n], m_dram[t, :, 0:n]).then_inc(mask_in[t % 2], 16)

                def load_q(t):
                    if t >= NT:
                        return
                    if t >= 1:
                        sp.wait_ge(q_split, 2 * t)
                    for kv in range(NKV):
                        for half in range(2):
                            sp.dma_start(q[half * HD:(half + 1) * HD, kv],
                                         q_dram[kv * HD:(kv + 1) * HD, :, t * P:(t + 1) * P]).then_inc(q_in, 16)

                sp.dma_start(onehot, A["bucket_onehot"]).then_inc(bias_in, 16)
                sp.dma_start(relb[:], A["rel_bias"]).then_inc(bias_in, 16)
                load_q(0)
                sp.wait_ge(ck_zeroed, 2)
                sp.dma_start(ck[:, 0:PAST // P, :], A["cache_k"][0, 0].rearrange("(j p) k d -> p j (k d)", p=P))\
                  .then_inc(ck_in, 16)
                sp.dma_start(ck[0:DEC, PAST // P, :], A["new_k_sample"][0, 0].rearrange("t k d -> t (k d)"))\
                  .then_inc(ck_in, 16)
                for kv in range(NKV):
                    sp.dma_start(vx[:, :, 2 * kv, :],
                                 A["new_v_prompt"][0, 0, :, kv].rearrange("(j p) d -> p j d", p=P)).then_inc(v_in, 16)
                sp.wait_ge(ckt_full, 3)
                load_S(FIRST)
                sp.wait_ge(k_low, 2)
                sp.dma_start(k2[0][HD:P, :].bitcast(F32), klow[0:HD, :].bitcast(F32)).then_inc(k_moved, 16)
                sp.dma_start(k2[1][0:HD, :].bitcast(F32), klow[HD:P, :].bitcast(F32)).then_inc(k_moved, 16)
                sp.wait_ge(g_exp, 2)
                sp.dma_start(g_dram, G.rearrange("h (a n) -> h a n", a=1).broadcast_to([NH, P, GLEN]))\
                  .then_inc(bias_out, 16)
                load_q(1)
                sp.wait_ge(bias_out, 16)
                sp.dma_start(EB[:], bass.AP(g_dram.tensor, P - 1, [[GLEN - 1, P], [P * GLEN, NH], [1, BIAS_W]]))\
                  .then_inc(eb_in, 16)
                sp.wait_ge(ks_lowered, 3)
                for part, swap in ((ks_high, 0), (ks_low, 1)):
                    for kv in range(NKV):
                        at = (kv ^ swap) * HD
                        sp.dma_start(k_dram[kv, at:at + HD, :], part[kv * HD:(kv + 1) * HD, :].bitcast(F32))\
                          .then_inc(ks_out, 16)
                sp.wait_ge(ks_out, 64)
                sp.dma_start(wout[:], A["w_out"][0].rearrange("(c p) n -> p c n", p=P)).then_inc(wout_in, 16)
                sp.dma_start(gpost[:], A["g_post"].broadcast_to([P, D])).then_inc(wout_in, 16)

                for p in range(NGR + 2):
                    if p == NGR - 1:
                        sp.wait_ge(pv_step, last_fl(ST - 1) + 1)
                        for kv in range(NKV):
                            sp.dma_start(k2[kv][:, 0:NSK * P].bitcast(F32), k_dram[kv]).then_inc(ks_in, 16)
                            sp.dma_start(vx[:, 0:PAST // P, 2 * kv, :],
                                         A["cache_v"][0, 0, :, kv].rearrange("(j p) d -> p j d", p=P))\
                              .then_inc(ks_in, 16)
                            sp.dma_start(vx[0:DEC, PAST // P, 2 * kv, :], A["new_v_sample"][0, 0, :, kv])\
                              .then_inc(ks_in, 16)
                    if p >= FIRST:
                        load_S(p + 1)
                    for t in group(p - 2):
                        sp.wait_ge(res_done, t + 1)
                        if t < NPT:
                            sp.dma_start(A["y_prompt"][0, t * P:(t + 1) * P, :], osb[:, t % 2, :])\
                              .then_inc(y_out[t % 2], 16)
                        else:
                            sp.dma_start(A["y_sample"][0], osb[0:DEC, t % 2, :]).then_inc(y_out[t % 2], 16)
                    for t in group(p - 1):
                        if t >= 2:
                            sp.wait_ge(res_done, t - 1)
                        if t < NPT:
                            sp.dma_start(xr[:, t % 2, :], A["x_prompt"][0, t * P:(t + 1) * P, :])\
                              .then_inc(xr_in[t % 2], 16)
                        else:
                            sp.dma_start(xr[0:DEC, t % 2, :], A["x_sample"][0]).then_inc(xr_in[t % 2], 16)
                    for t in group(p):
                        if t >= 2:
                            sp.wait_ge(yT_done, t - 1)
                        sp.dma_start(gb[:, t % 2].rearrange("p (j n) -> p j n", j=GRP),
                                     gb_dram[:, :, t * P:(t + 1) * P]).then_inc(gb_in[t % 2], 16)
                    for t in group(p):
                        if t >= 2:
                            sp.wait_ge(o_full, 2 * (t - 1))
                        sp.dma_start(ma[:, t % 2], ma_dram[:, :, t * P:(t + 1) * P]).then_inc(ma_in[t % 2], 16)
                    for t in group(p + 1):
                        load_mask(t)
                        load_q(t)
                for i in range(2):
                    sp.wait_ge(y_out[i], 16 * len(range(i, NT, 2)))

            @block.gpsimd
            def _(pool):
                def low(t):
                    pool.wait_ge(q_split, 2 * t + 1)
                    if t >= 2:
                        pool.wait_ge(fl_full, last_fl(t - 2) + 1)
                    pool.tensor_tensor(ql[:, t % 2], q[:], qh[:, t % 2].bitcast(F32), ALU.subtract)\
                        .then_inc(q_split, 1)

                pool.memset(ck[:, PAST // P, :], 0.0).then_inc(ck_zeroed, 1)
                pool.memset(vx[:], 2.0).then_inc(ck_zeroed, 1)
                for t in range(TOPK // P):
                    n = key_tiles(t) * P
                    pool.memset(mask[:, t, 0:n], 0.0).then_inc(plain_mask, 1)
                    pool.wait_ge(plain_mask, 2 * t + 1)
                    pool.memset(mask[0:CHUNK, t, n - CHUNK:n], MASKED).then_inc(plain_mask, 1)
                for t in range(EARLY[-1] + 1, NT):
                    pool.memset(enough[:, t:t + 1], key_tiles(t) * P - 2.0 * TOPK + 1.5).then_inc(enough_set, 1)
                low(0)
                low(1)
                pool.wait_ge(eb_in, 16)
                for p in range(NGR + 2):
                    for t in group(p - 2):
                        r = P if t < NPT else DEC
                        pool.wait_ge(xr_in[t % 2], 16 * (t // 2 + 1))
                        pool.wait_ge(post_done, t + 1)
                        pool.tensor_tensor(osb[0:r, t % 2, :], osb[0:r, t % 2, :], xr[0:r, t % 2, :], ALU.add)\
                            .then_inc(res_done, 1)
                    for t in group(p - 1):
                        pool.wait_ge(recip_done, t + 1)
                        pool.tensor_tensor(osum[:, t % 2], osum[:, t % 2], den[:, t % 2], ALU.mult)\
                            .then_inc(mean_done, 1)
                        pool.wait_ge(gb_in[t % 2], 16 * (t // 2 + 1))
                        if t >= 2:
                            pool.wait_ge(o_full, 2 * (t - 1))
                        pool.wait_ge(mean_done, t + 1)
                        pool.tensor_tensor(yT[:, t % 2].rearrange("p j n -> p (j n)"), osum[:, t % 2], gb[:, t % 2],
                                           ALU.mult).then_inc(yT_done, 1)
                    for t, kv, kt in jobs(p):
                        if near(t, kt):
                            k = fl[t, kv, kt]
                            off = (place_of(t) - kt) * P
                            pool.wait_ge(fl_free, k + 1)
                            pool.tensor_tensor(E[:, k % 4], E[:, k % 4],
                                               EB[:, kv * GRP:(kv + 1) * GRP, off:off + P], ALU.mult)\
                                .then_inc(biased, 1)
                        if (kv, kt) == (NKV - 1, key_tiles(t) - 1) and t + 2 < NT:
                            low(t + 2)

            @block.scalar
            def _(act):
                def high(t):
                    act.wait_ge(q_in, 64 * (t + 1))
                    if t >= 2:
                        act.wait_ge(fl_full, last_fl(t - 2) + 1)
                    act.activation(qh[:, t % 2], q[:], ACT.Copy).then_inc(q_split, 1)

                def take_sums(t, kv):
                    act.wait_ge(pv_step, last_fl(t, kv) + 1)
                    if t >= 2:
                        act.wait_ge(yT_done, t - 1)
                    own = slice(kv * HD, (kv + 1) * HD)
                    other = slice((1 - kv) * HD, (2 - kv) * HD)
                    act.activation(osum[own, t % 2], wide[0][own, kv * 512:(kv + 1) * 512], ACT.Copy)\
                       .then_inc(sums_out, 1)
                    act.activation(den[own, t % 2], wide[0][other, kv * 512:(kv + 1) * 512], ACT.Copy)\
                       .then_inc(sums_out, 1)

                act.activation(k2[0][0:HD, :], kT[0:HD, :], ACT.Copy).then_inc(k_split, 1)
                act.activation(k2[1][HD:P, :], kT[HD:P, :], ACT.Copy).then_inc(k_split, 1)
                act.wait_ge(g_full, 1)
                act.wait_ge(nfar_done, 1)
                act.activation(G[:, 0:512], banks[0][0:NH, :], ACT.Exp, bias=nfar[:]).then_inc(g_exp, 1)
                act.activation(G[:, 512:GLEN], banks[1][0:NH, 0:GLEN - 512], ACT.Exp, bias=nfar[:]).then_inc(g_exp, 1)
                high(0)
                for i, (src, a, b) in enumerate(sample_keys):
                    act.wait_ge(ckt_full, i + 1)
                    act.activation(ks_high[:, a * P:b * P], src[:, 0:(b - a) * P], ACT.Copy).then_inc(ks_split, 1)
                high(1)
                done = 0

                def magnify(p):
                    for i, t in enumerate(group(p)):
                        w = key_tiles(t) * P
                        act.wait_ge(S_in[i], 16 * (p - FIRST + 1))
                        act.activation(B.near[:, i, 0:w], S[:, i, 0:w], ACT.Copy, scale=B.scale[:, i:i + 1])\
                           .then_inc(halved, 1)

                def halve_first(p, r):
                    nonlocal done
                    for i, t in enumerate(group(p)):
                        w = key_tiles(t) * P
                        act.wait_ge(halved, done)
                        act.activation(act_junk[:, 0:w], B.near[:, i, 0:w], ACT.Sign, bias=minus_cand[:, i:i + 1],
                                       accum_out=act_sum[:, i:i + 1]).then_inc(halved, 1)
                        done += 1
                    for i, t in enumerate(group(p)):
                        act.wait_ge(halved, done)
                        act.activation(act_side[:, i:i + 1], act_sum[:, i:i + 1], ACT.Sign, bias=enough[:, t:t + 1])\
                           .then_inc(halved, 1)
                        done += 1
                    for i, t in enumerate(group(p)):
                        act.wait_ge(halved, done)
                        act.activation(minus_cand[:, i:i + 1], act_side[:, i:i + 1], ACT.Identity,
                                       scale=-REACH / 2.0 ** (r + 1), bias=minus_cand[:, i:i + 1]).then_inc(halved, 1)
                        done += 1

                for p in range(NGR + 1):
                    ahead = p + 1 if searched(p + 1) and p >= FIRST else None
                    if ahead:
                        act.wait_ge(first_ready, p - FIRST + 1)
                        magnify(ahead)
                        done += len(group(ahead))
                        halve_first(ahead, 0)
                    rounds = list(range(1, ACT_ROUNDS))
                    for t in group(p - 1):
                        if t == 0:
                            act.wait_ge(k_moved, 32)
                        for i in range(2):
                            act.wait_ge(o_full, 2 * t + i + 1)
                            if 2 * t + i:
                                act.wait_ge(o_free, 4 * t + 2 * i)
                            act.activation(sq[:], wide[1][:, i * 512:(i + 1) * 512], ACT.Square,
                                           accum_out=ss2[:, t, i:i + 1]).then_inc(o_free, 1)
                            if i == 0 and t >= 2:
                                act.wait_ge(y_out[t % 2], 16 * (t // 2))
                            act.activation(osb[:, t % 2, i * 512:(i + 1) * 512], wide[1][:, i * 512:(i + 1) * 512],
                                           ACT.Copy).then_inc(o_free, 1)
                            if ahead and rounds:
                                halve_first(ahead, rounds.pop(0))
                    while ahead and rounds:
                        halve_first(ahead, rounds.pop(0))
                    waiting = []
                    for t, kv, kt in jobs(p):
                        k = fl[t, kv, kt]
                        act.wait_ge(fl_full, k + 1)
                        if k >= 4:
                            act.wait_ge(pv_step, k - 3)
                        act.activation(E[:, k % 4], banks[2 + k % 2][:].rearrange("p (j n) -> p j n", j=GRP),
                                       ACT.Exp).then_inc(fl_free, 1)
                        while waiting and last_fl(*waiting[0]) <= k - 2:
                            take_sums(*waiting.pop(0))
                        if kt == key_tiles(t) - 1:
                            waiting.append((t, kv))
                            if kv == NKV - 1 and t + 2 < NT:
                                high(t + 2)
                    for w in waiting:
                        take_sums(*w)

            @block.tensor
            def _(pe):
                pe.wait_ge(bias_in, 32)
                pe.matmul(banks[0][0:NH, :], relb[:], onehot[:, 0:512], start=True, stop=True)
                pe.matmul(banks[1][0:NH, 0:GLEN - 512], relb[:], onehot[:, 512:GLEN], start=True, stop=True)\
                  .then_inc(g_full, 1)
                pe.wait_ge(ck_in, 32)
                for dst, a, b in sample_keys:
                    for j in range(a, b):
                        tr = pe.transpose(dst[:, (j - a) * P:(j - a + 1) * P], ck[:, j, :], identf[:])
                    tr.then_inc(ckt_full, 1)
                pe.wait_ge(g_exp, 2)
                pe.wait_ge(ks_lowered, 3)
                pe.wait_ge(k_split, 2)
                pe.wait_ge(k_moved, 32)

                def max_logits(t, h, c):
                    if h == 0 and c == 0:
                        pe.wait_ge(q_split, 2 * t + 1)
                        if t == ST:
                            pe.wait_ge(ks_in, 96)
                    k = fx[t, h, c]
                    if k >= 2:
                        pe.wait_ge(fx_free, k - 1)
                    kv, j = divmod(h, GRP)
                    a, b = chunks(t)[c]
                    pe.matmul(banks[k % 2][:, 0:b - a], qh[:, t % 2, kv, j, :], k2[kv][:, a:b], start=True, stop=True)\
                      .then_inc(fx_full, 1)

                def logits(t, kv, kt):
                    k = fl[t, kv, kt]
                    if kv == 0 and kt == 0:
                        pe.wait_ge(q_split, 2 * t + 2)
                        pe.wait_ge(shift_done, t + 1)
                    if k >= 2:
                        pe.wait_ge(fl_free, k - 1)
                    bank = banks[2 + k % 2][:].rearrange("p (j n) -> p j n", j=GRP)
                    keys = k2[kv][:, kt * P:(kt + 1) * P]
                    pe.matmul(bank, keys, qh[:, t % 2, kv], start=True, stop=False)
                    pe.matmul(bank, keys, ql[:, t % 2, kv], start=False, stop=False)
                    pe.matmul(bank, mask[:, t % 2, kt * P:(kt + 1) * P],
                              identb[:].rearrange("p (a n) -> p a n", a=1).broadcast_to([P, GRP, P]),
                              start=False, stop=False)
                    pe.matmul(bank, onesb[:], shift[:, t % 2, kv * GRP:(kv + 1) * GRP], start=False, stop=True)\
                      .then_inc(fl_full, 1)

                def weighted_values(t, kv, kt):
                    k = fl[t, kv, kt]
                    if near(t, kt):
                        pe.wait_ge(biased, near_count[t, kv, kt])
                    else:
                        pe.wait_ge(fl_free, k + 1)
                    if kt == 0 and t >= 1:
                        pe.wait_ge(sums_out, 4 * (t - 1) + 2 * (kv + 1))
                    pe.matmul(wide[0][:, kv * 512:(kv + 1) * 512], vx[:, kt, kv:kv + 2, :].rearrange("p a d -> p (a d)"),
                              E[:, k % 4].rearrange("p j n -> p (j n)"), start=(kt == 0),
                              stop=(kt == key_tiles(t) - 1)).then_inc(pv_step, 1)

                def attention(p):
                    todo = jobs(p)
                    if p == 0:
                        pe.wait_ge(v_in, 32)
                    for i in range(len(todo) + 2):
                        if i < len(todo):
                            logits(*todo[i])
                        if 2 <= i:
                            weighted_values(*todo[i - 2])

                def output(t, i, c):
                    if i == 0 and c == 0:
                        pe.wait_ge(wout_in, 32)
                        pe.wait_ge(ma_in[t % 2], 16 * (t // 2 + 1))
                    if c == 0 and t >= 1:
                        pe.wait_ge(o_free, 4 * (t - 1) + 2 * (i + 1))
                    if c == NG:
                        pe.wait_ge(yT_done, t + 1)
                    stat = ma[:, t % 2, c, :] if c < NG else yT[:, t % 2, c - NG, :]
                    mm = pe.matmul(wide[1][:, i * 512:(i + 1) * 512], stat, wout[:, c, i * 512:(i + 1) * 512],
                                   start=(c == 0), stop=(c == DC - 1))
                    if c == DC - 1:
                        mm.then_inc(o_full, 1)

                for p in range(NGR + 1):
                    outs = [(t, i, c) for t in group(p - 1) for i in range(2) for c in range(DC)]
                    maxs = [(t, h, c) for t in group(p) for h in range(NH) for c in range(len(chunks(t)))]
                    if p >= NGR - 1:
                        for o in outs:
                            output(*o)
                        outs = []
                    for i, x in enumerate(maxs):
                        max_logits(*x)
                        if i % 2 and i // 2 < len(outs):
                            output(*outs[i // 2])
                    for o in outs[len(maxs) // 2:]:
                        output(*o)
                    attention(p)

            @block.vector
            def _(dve):
                n = 0

                def link(ins):
                    nonlocal n
                    ins.then_inc(dk, 1)
                    n += 1

                dve.wait_ge(k_split, 2)
                dve.tensor_tensor(klow[0:HD, :], kT[0:HD, :], k2[0][0:HD, :].bitcast(F32), ALU.subtract)\
                   .then_inc(k_low, 1)
                dve.tensor_tensor(klow[HD:P, :], kT[HD:P, :], k2[1][HD:P, :].bitcast(F32), ALU.subtract)\
                   .then_inc(k_low, 1)
                dve.wait_ge(g_full, 1)
                dve.tensor_scalar(nfar[:], banks[1][0:NH, GLEN - 513:GLEN - 512], -1.0, None, ALU.mult)\
                   .then_inc(nfar_done, 1)
                for i, (src, a, b) in enumerate(sample_keys):
                    dve.wait_ge(ks_split, i + 1)
                    dve.tensor_tensor(ks_low[:, a * P:b * P], src[:, 0:(b - a) * P],
                                      ks_high[:, a * P:b * P].bitcast(F32), ALU.subtract).then_inc(ks_lowered, 1)
                dve.wait_ge(bias_out, 16)

                def continue_search(p):
                    nonlocal n
                    dve.wait_ge(halved, sum(len(group(u)) * (1 + 3 * ACT_ROUNDS) for u in range(FIRST + 1, p + 1)))
                    cols = slice(0, len(group(p)))
                    link(dve.tensor_scalar(B.cand[:, cols], minus_cand[:, cols], -1.0, None, ALU.mult))
                    link(dve.memset(B.width[:], 2.0 * REACH / 2.0 ** ACT_ROUNDS))
                    n = halve(dve, dk, n, B, [key_tiles(t) * P for t in group(p)], ROUNDS[0] - ACT_ROUNDS)

                def open_search(p, level):
                    nonlocal n
                    tiles = group(p)
                    if level == 0:
                        for i in range(len(tiles)):
                            dve.wait_ge(S_in[i], 16 * (p - FIRST + 1))
                    n = open_level(dve, dk, n, B, level, top[:, tiles[0]:tiles[-1] + 1],
                                   [S[:, i, 0:key_tiles(t) * P] for i, t in enumerate(tiles)])

                def narrow(p, level):
                    nonlocal n
                    n = halve(dve, dk, n, B, [key_tiles(t) * P for t in group(p)], ROUNDS[level])

                def set_mask(t):
                    nonlocal n
                    w = key_tiles(t) * P
                    if t > group(FIRST)[0]:
                        dve.wait_ge(mask_done, t - group(FIRST)[0])
                    n = choose(dve, dk, n, B, t % 2, w)
                    dve.wait_ge(fl_full, last_fl(t - 2) + 1)
                    dve.tensor_scalar(mask[:, t % 2, 0:w], B.reach[:, 0:w], MASKED, None, ALU.mult)\
                       .then_inc(mask_done, 1)

                def maxima(t):
                    nonlocal n
                    if t < TOPK // P:
                        dve.wait_ge(plain_mask, 2 * (t + 1))
                    elif t in EARLY:
                        dve.wait_ge(mask_in[t % 2], 16 * ((t - EARLY[0]) // 2 + 1))
                    else:
                        dve.wait_ge(mask_done, t - group(FIRST)[0] + 1)
                    nc_ = len(chunks(t))
                    for h in range(NH):
                        for c, (a, b) in enumerate(chunks(t)):
                            k = fx[t, h, c]
                            dve.wait_ge(fx_full, k + 1)
                            if k >= 2:
                                dve.wait_ge(fx_free, k - 1)
                            dve.tensor_tensor_reduce(junk[:, k % 2 * 512:k % 2 * 512 + b - a], banks[k % 2][:, 0:b - a],
                                                     mask[:, t % 2, a:b], 1.0, LEAST, ALU.add, ALU.max,
                                                     mxp[:, h, c:c + 1]).then_inc(fx_free, 1)
                    dve.wait_ge(fx_free, last_fx(t) + 1)
                    link(dve.tensor_reduce(nmax[:], mxp[:, :, 0:nc_], AX.X, ALU.max, negate=True))
                    dve.wait_ge(dk, n)
                    if t >= 2:
                        dve.wait_ge(fl_full, last_fl(t - 2) + 1)
                    for h in range(NH):
                        ins = dve.tensor_scalar(shift[:, t % 2, h, :], identb[:], nmax[:, h:h + 1], None, ALU.mult)
                    ins.then_inc(shift_done, 1)

                def invert_sums(t):
                    dve.wait_ge(sums_out, 4 * (t + 1))
                    dve.reciprocal(den[:, t % 2], den[:, t % 2]).then_inc(recip_done, 1)

                def post_norm(tiles):
                    nonlocal n
                    if not tiles:
                        return
                    a, b = tiles[0], tiles[-1] + 1
                    m = b - a
                    dve.wait_ge(o_free, 4 * b)
                    link(dve.tensor_tensor(root[:, 3, 0:m], ss2[:, a:b, 0], ss2[:, a:b, 1], ALU.add))
                    dve.wait_ge(dk, n)
                    n = inverse_root(dve, dk, n, root[:, 0, 0:m], root[:, 1, 0:m], root[:, 2, 0:m], root[:, 3, 0:m],
                                     1.0 / D)
                    dve.wait_ge(wout_in, 32)
                    for t in tiles:
                        dve.scalar_tensor_tensor(osb[:, t % 2], osb[:, t % 2], root[:, 1, t - a:t - a + 1], gpost[:],
                                                 ALU.mult, ALU.mult).then_inc(post_done, 1)

                def last_level(p):
                    open_search(p, 2)
                    narrow(p, 2)
                    dve.wait_ge(dk, n)
                    dve.memset(B.width[:], 0.0).then_inc(S_used, 1)
                    dve.wait_ge(S_used, p - FIRST + 1)

                for p in range(NGR + 2):
                    before = group(p - 1)
                    if FIRST - 2 <= p < FIRST:
                        open_search(FIRST, p - FIRST + 2)
                        narrow(FIRST, p - FIRST + 2)
                    elif FIRST < p < NGR:
                        continue_search(p)
                    if FIRST < p < NGR:
                        open_search(p, 1)
                        narrow(p, 1)
                    post_norm(group(p - 2))
                    for t in before[:1]:
                        invert_sums(t)
                    if searched(p):
                        last_level(p)
                        set_mask(group(p)[0])
                    for t in before[1:]:
                        invert_sums(t)
                    if searched(p):
                        for t in group(p)[1:]:
                            set_mask(t)
                        if searched(p + 1):
                            ahead = group(p + 1)
                            dve.wait_ge(mask_done, ahead[0] - group(FIRST)[0])
                            n = first_units(dve, dk, n, B, top[:, ahead[0]:ahead[-1] + 1])
                            dve.wait_ge(dk, n)
                            dve.memset(minus_cand[:], 0.0).then_inc(first_ready, 1)
                    for t in group(p):
                        maxima(t)


INPUTS = ["x_prompt", "x_sample", "cache_k", "cache_v", "cache_kidx", "state_pool", "rel_bias", "g_pre", "w_in",
          "w_pool", "pool_scale", "w_out", "g_post"]
OUTPUTS = {
    "y_prompt": (1, SEQ, D), "y_sample": (1, DEC, D),
    "new_k_prompt": (1, 1, SEQ, NKV, HD), "new_v_prompt": (1, 1, SEQ, NKV, HD),
    "new_kidx_prompt": (1, 1, SEQ, DI), "new_pool_prompt": (1, 1, HIST, DPOOL),
    "new_k_sample": (1, 1, DEC, NKV, HD), "new_v_sample": (1, 1, DEC, NKV, HD),
    "new_kidx_sample": (1, 1, DEC, DI), "new_pool_sample": (1, 1, HIST, DPOOL),
}


def tables():
    rel = P - 1 - np.arange(GLEN)
    half = NBUCKETS // 2
    exact = half // 2
    n = np.abs(rel)
    large = exact + (np.log(np.maximum(n, 1).astype(np.float32) / exact) / np.log(1024 / exact)
                     * (half - exact)).astype(np.int32)
    bucket = np.where(rel > 0, half, 0) + np.where(n < exact, n, np.minimum(large, half - 1))
    assert bucket[-1] == half - 1 and n[-1] >= 558
    onehot = (bucket[None, :] == np.arange(NBUCKETS)[:, None]).astype(np.float32)
    fix = np.ones((P, NG, 16), np.float32)
    for g in range(NG):
        w = 2 << g
        fix[:, g, :] = w / np.minimum(w, np.arange(16) + 1)
    return {"bucket_onehot": onehot, "pool_fix": fix}


def layout(inputs):
    arrays = {n: np.ascontiguousarray(inputs[n]) for n in INPUTS} | tables()
    for n in ("g_pre", "pool_scale"):
        arrays[n] = np.ascontiguousarray(arrays[n].reshape(-1, P).T)
    w = arrays["w_in"]

    def ordered(columns):
        return columns.reshape(1, D, NKV, GRP, HD).transpose(0, 1, 3, 2, 4).reshape(1, D, NH * HD)

    arrays["w_in"] = np.concatenate([w[:, :, :C_Q], ordered(w[:, :, C_Q:C_K]), w[:, :, C_K:C_GB],
                                     ordered(w[:, :, C_GB:])], axis=2)
    w = arrays["w_out"]
    arrays["w_out"] = np.concatenate(
        [w[:, :DPOOL], ordered(w[:, DPOOL:].transpose(0, 2, 1)).transpose(0, 2, 1)], axis=1)
    return arrays


def program(nc, arrays):
    A = {n: nc.dram_tensor(n, a.shape, mybir.dt.from_np(a.dtype), kind="ExternalInput").ap() for n, a in arrays.items()}
    for n, shape in OUTPUTS.items():
        A[n] = nc.dram_tensor(n, shape, F32, kind="ExternalOutput").ap()
    build(nc, A)


def kernel(**inputs):
    import concourse.bacc as bacc
    from concourse.bass_utils import run_bass_kernel_spmd

    nc = bacc.Bacc("TRN2", target_bir_lowering=False, num_devices=1)
    arrays = layout(inputs)
    program(nc, arrays)
    r = run_bass_kernel_spmd(nc, [arrays], core_ids=[0])
    return tuple(r.results[0][n] for n in OUTPUTS)
```
